# Optimizing a Trainium2 kernel written in Bass

```python
import jax, jax.numpy as jnp
from jax import lax
import numpy as np

D_MODEL = 1024
BATCH = 1
SEQ = 256
DEPTH = 2

GRID_W = 64
CTX_LEN = 256
N_MIXERS = 2
N_POOL_LAYERS = (DEPTH + 1) // 2
N_DELTA_LAYERS = DEPTH // 2
NORM_EPS = 1e-6
POOL_WINDOWS = (2, 4, 8, 16)
N_POOL_GROUPS = 4
POOL_GROUP = D_MODEL // N_POOL_GROUPS
DN_HEADS = 8
DN_HEAD_DIM = D_MODEL // DN_HEADS
DN_CONV = 5
DN_CHUNK = 64
PEER_HEADS = 8
PEER_KEY_DIM = 256
PEER_N_KEYS = 128
PEER_N_EXPERTS = PEER_N_KEYS ** 2
PEER_TOPK = 16
PEER_BLOCK = 128

kernel_name = "hybrid_pool_deltanet_peer_dit"

def rmsnorm(h, gain):
    hf = h.astype(jnp.float32)
    y = hf * lax.rsqrt(jnp.mean(hf * hf, axis=-1, keepdims=True) + NORM_EPS)
    return (y * gain.astype(jnp.float32)).astype(h.dtype)

def modulate(h, gain, shift, scale):
    return rmsnorm(h, gain) * (1.0 + scale) + shift

def box_mean(u, axis, w):
    n = u.shape[axis]
    cs = jnp.cumsum(u, axis=axis)
    cs = jnp.concatenate([jnp.zeros_like(lax.slice_in_dim(cs, 0, 1, axis=axis)), cs], axis=axis)
    t = jnp.arange(n)
    lo = jnp.clip(t - w // 2, 0, n)
    hi = jnp.clip(t - w // 2 + w, 0, n)
    s = jnp.take(cs, hi, axis=axis) - jnp.take(cs, lo, axis=axis)
    shape = [1] * u.ndim
    shape[axis] = n
    return s / (hi - lo).astype(u.dtype).reshape(shape)

def pool_mixer(h, w_groups, scale, on_grid):
    B, L, D = h.shape
    hf = h.astype(jnp.float32).reshape(B, L, N_POOL_GROUPS, POOL_GROUP)
    if on_grid:
        rows = L // GRID_W
        hf = hf.reshape(B, rows, GRID_W, N_POOL_GROUPS, POOL_GROUP)
    groups = []
    for gi, w in enumerate(POOL_WINDOWS):
        xg = hf[..., gi, :]
        pooled = box_mean(box_mean(xg, 1, w), 2, w) if on_grid else box_mean(xg, 1, w)
        groups.append(pooled - xg)
    p = jnp.stack(groups, axis=-2).reshape(B, L, N_POOL_GROUPS, POOL_GROUP).astype(h.dtype)
    y = jnp.einsum('blgi,gio->blgo', p, w_groups).reshape(B, L, D)
    return y * scale

def short_conv(u, w):
    ch = u.shape[-1]
    y = lax.conv_general_dilated(u, w[:, None, :].astype(u.dtype), window_strides=(1,),
                                 padding=[(DN_CONV // 2, DN_CONV // 2)],
                                 dimension_numbers=('NWC', 'WIO', 'NWC'), feature_group_count=ch)
    return jax.nn.silu(y)

def l2norm(u):
    return u * lax.rsqrt(jnp.sum(u * u, axis=-1, keepdims=True) + NORM_EPS)

def dn_project(h, w_in, conv_w, a_log, dt_bias):
    B, L, D = h.shape
    p = h @ w_in
    qkv = short_conv(p[..., :3 * D], conv_w).astype(jnp.float32)
    qkv = qkv.reshape(B, L, 3, DN_HEADS, DN_HEAD_DIM).transpose(2, 0, 3, 1, 4)
    q = l2norm(qkv[0]) * (DN_HEAD_DIM ** -0.5)
    k = l2norm(qkv[1])
    v = qkv[2]
    z = p[..., 3 * D:4 * D]
    ab = p[..., 4 * D:].astype(jnp.float32).reshape(B, L, 2, 2, DN_HEADS).transpose(2, 3, 0, 4, 1)
    g = -jnp.exp(a_log.astype(jnp.float32))[:, None, :, None] * jax.nn.softplus(
        ab[:, 0] + dt_bias.astype(jnp.float32)[:, None, :, None])
    beta = jax.nn.sigmoid(ab[:, 1])
    return q, k, v, z, g, beta

def gated_delta_chunk(q, k, v, beta, g, s0, with_output):
    B, H, L, dk = q.shape
    dv = v.shape[-1]
    n = L // DN_CHUNK
    q = q.reshape(B, H, n, DN_CHUNK, dk)
    k = k.reshape(B, H, n, DN_CHUNK, dk)
    v = v.reshape(B, H, n, DN_CHUNK, dv)
    beta = beta.reshape(B, H, n, DN_CHUNK)
    g = jnp.cumsum(g.reshape(B, H, n, DN_CHUNK), axis=-1)
    kb = k * beta[..., None]
    vb = v * beta[..., None]
    idx = jnp.arange(DN_CHUNK)
    incl = idx[:, None] >= idx[None, :]
    strict = idx[:, None] > idx[None, :]
    decay = jnp.exp(jnp.where(incl, g[..., :, None] - g[..., None, :], -jnp.inf))
    a = jnp.where(strict, jnp.einsum('bhnid,bhnjd->bhnij', kb, k) * decay, 0.0)
    eye = jnp.eye(DN_CHUNK, dtype=q.dtype)
    t_inv = lax.linalg.triangular_solve(eye + a, jnp.broadcast_to(eye, a.shape), left_side=True,
                                        lower=True, unit_diagonal=True)
    u = t_inv @ vb
    w = t_inv @ (kb * jnp.exp(g)[..., None])
    kg = k * jnp.exp(g[..., -1:] - g)[..., None]
    glast = jnp.exp(g[..., -1])
    seq_first = lambda t: jnp.moveaxis(t, 2, 0)
    if with_output:
        attn = jnp.einsum('bhnid,bhnjd->bhnij', q, k) * decay
        qg = q * jnp.exp(g)[..., None]
        xs = tuple(seq_first(t) for t in (kg, u, w, glast, qg, attn))
    else:
        xs = tuple(seq_first(t) for t in (kg, u, w, glast))

    def step(s, inp):
        kg_i, u_i, w_i, gl_i = inp[:4]
        v_new = u_i - w_i @ s
        s_new = s * gl_i[..., None, None] + jnp.swapaxes(kg_i, -1, -2) @ v_new
        if with_output:
            qg_i, attn_i = inp[4:]
            return s_new, qg_i @ s + attn_i @ v_new
        return s_new, None

    s_fin, o = lax.scan(step, s0, xs)
    if with_output:
        o = jnp.moveaxis(o, 0, 2).reshape(B, H, L, dv)
    return o, s_fin

def dn_output(o, z, norm_g, w_out):
    B, H, L, dh = o.shape
    o = o.transpose(0, 2, 1, 3)
    o = o * lax.rsqrt(jnp.mean(o * o, axis=-1, keepdims=True) + NORM_EPS) * norm_g.astype(jnp.float32)
    o = o * jax.nn.silu(z.astype(jnp.float32).reshape(B, L, H, dh))
    return o.reshape(B, L, H * dh).astype(z.dtype) @ w_out

def delta_mixer(hx, hc, w_in, conv_w, a_log, dt_bias, norm_g, w_out, ctx_out):
    qx, kx, vx, zx, gx, bx = dn_project(hx, w_in, conv_w, a_log, dt_bias)
    qc, kc, vc, zc, gc, bc = dn_project(hc, w_in, conv_w, a_log, dt_bias)
    B = hx.shape[0]
    s0 = jnp.zeros((B, DN_HEADS, DN_HEAD_DIM, DN_HEAD_DIM), jnp.float32)
    flip = lambda t: jnp.flip(t, axis=2)
    oc_f, sc_f = gated_delta_chunk(qc, kc, vc, bc[0], gc[0], s0, ctx_out)
    ox_f, _ = gated_delta_chunk(qx, kx, vx, bx[0], gx[0], sc_f, True)
    oc_b, sc_b = gated_delta_chunk(flip(qc), flip(kc), flip(vc), flip(bc[1]), flip(gc[1]), s0, ctx_out)
    ox_b, _ = gated_delta_chunk(flip(qx), flip(kx), flip(vx), flip(bx[1]), flip(gx[1]), sc_b, True)
    yx = dn_output(ox_f + flip(ox_b), zx, norm_g, w_out)
    yc = dn_output(oc_f + flip(oc_b), zc, norm_g, w_out) if ctx_out else None
    return yx, yc

def peer(h, wq, keys, u_tab, v_tab):
    B, L, D = h.shape
    T = B * L
    hf = h.reshape(T, D)
    q = (hf @ wq).reshape(T, PEER_HEADS, 2, PEER_KEY_DIM // 2)
    s = jnp.einsum('thpd,hpkd->thpk', q, keys).astype(jnp.float32)
    s1, i1 = lax.top_k(s[:, :, 0], PEER_TOPK)
    s2, i2 = lax.top_k(s[:, :, 1], PEER_TOPK)
    cand = (s1[..., :, None] + s2[..., None, :]).reshape(T, PEER_HEADS, PEER_TOPK * PEER_TOPK)
    cidx = (i1[..., :, None] * PEER_N_KEYS + i2[..., None, :]).reshape(T, PEER_HEADS, PEER_TOPK * PEER_TOPK)
    sc, pos = lax.top_k(cand, PEER_TOPK)
    nb = T // PEER_BLOCK
    eidx = jnp.take_along_axis(cidx, pos, axis=-1).reshape(nb, PEER_BLOCK, PEER_HEADS * PEER_TOPK)
    gate = jax.nn.softmax(sc, axis=-1).astype(h.dtype).reshape(nb, PEER_BLOCK, PEER_HEADS * PEER_TOPK)
    xb = hf.reshape(nb, PEER_BLOCK, D)

    def block(args):
        xt, et, gt = args
        act = jax.nn.gelu(jnp.einsum('td,ted->te', xt, jnp.take(u_tab, et, axis=0)), approximate=False)
        return jnp.einsum('te,ted->td', gt * act, jnp.take(v_tab, et, axis=0))

    y = lax.map(block, (xb, eidx, gate))
    return y.reshape(B, L, D)

def setup_inputs(seed: int = 0) -> dict:
    key = jax.random.key(seed)
    ks = jax.random.split(key, 24)
    D = D_MODEL
    f32 = jnp.float32
    nrm = lambda k, shape, s: jax.random.normal(k, shape, f32) * s
    dt = jnp.exp(jax.random.uniform(ks[13], (N_DELTA_LAYERS, 2, DN_HEADS), f32,
                                    minval=float(np.log(1e-3)), maxval=float(np.log(1e-1))))
    return {
        "x": nrm(ks[0], (BATCH, SEQ, D), 1.0),
        "c": nrm(ks[1], (BATCH, D), 1.0),
        "ctx": nrm(ks[2], (BATCH, CTX_LEN, D), 1.0),
        "c_ctx": nrm(ks[3], (D,), 1.0),
        "mod_w": nrm(ks[4], (DEPTH, D, 6 * D), 0.5 * D ** -0.5),
        "mod_b": nrm(ks[5], (DEPTH, 6 * D), 0.02),
        "norm1_g": 1.0 + nrm(ks[6], (DEPTH, D), 0.02),
        "norm2_g": 1.0 + nrm(ks[7], (DEPTH, D), 0.02),
        "pool_w": nrm(ks[8], (N_POOL_LAYERS, N_POOL_GROUPS, POOL_GROUP, POOL_GROUP), POOL_GROUP ** -0.5),
        "pool_scale": 1.0 + nrm(ks[9], (N_POOL_LAYERS, D), 0.1),
        "dn_w_in": nrm(ks[10], (N_DELTA_LAYERS, D, 4 * D + 4 * DN_HEADS), D ** -0.5),
        "dn_conv_w": nrm(ks[11], (N_DELTA_LAYERS, DN_CONV, 3 * D), DN_CONV ** -0.5),
        "dn_a_log": jnp.log(jax.random.uniform(ks[12], (N_DELTA_LAYERS, 2, DN_HEADS), f32, minval=1.0, maxval=16.0)),
        "dn_dt_bias": dt + jnp.log(-jnp.expm1(-dt)),
        "dn_norm_g": 1.0 + nrm(ks[14], (N_DELTA_LAYERS, DN_HEAD_DIM), 0.02),
        "dn_w_out": nrm(ks[15], (N_DELTA_LAYERS, D, D), D ** -0.5),
        "peer_wq": nrm(ks[16], (DEPTH, D, PEER_HEADS * PEER_KEY_DIM), D ** -0.5),
        "peer_keys": nrm(ks[17], (DEPTH, PEER_HEADS, 2, PEER_N_KEYS, PEER_KEY_DIM // 2), (PEER_KEY_DIM // 2) ** -0.5),
        "peer_u": nrm(ks[18], (DEPTH, PEER_N_EXPERTS, D), D ** -0.5),
        "peer_v": nrm(ks[19], (DEPTH, PEER_N_EXPERTS, D), 0.5),
        "final_g": 1.0 + nrm(ks[20], (D,), 0.02),
    }

def reference(x, c, ctx, c_ctx, mod_w, mod_b, norm1_g, norm2_g, pool_w, pool_scale,
              dn_w_in, dn_conv_w, dn_a_log, dn_dt_bias, dn_norm_g, dn_w_out,
              peer_wq, peer_keys, peer_u, peer_v, final_g):
    hx, hc = x, ctx
    for i in range(DEPTH):
        last = i == DEPTH - 1
        is_pool = (i % N_MIXERS) == 0
        j = i // N_MIXERS
        mx = [m[:, None, :] for m in jnp.split(jax.nn.silu(c) @ mod_w[i] + mod_b[i], 6, axis=-1)]
        need_ctx = (not last) or (not is_pool)
        if need_ctx:
            mc = jnp.split(jax.nn.silu(c_ctx) @ mod_w[i] + mod_b[i], 6, axis=-1)
        ax = modulate(hx, norm1_g[i], mx[0], mx[1])
        if is_pool:
            hx = hx + mx[2] * pool_mixer(ax, pool_w[j], pool_scale[j], True)
            if not last:
                ac = modulate(hc, norm1_g[i], mc[0], mc[1])
                hc = hc + mc[2] * pool_mixer(ac, pool_w[j], pool_scale[j], False)
        else:
            ac = modulate(hc, norm1_g[i], mc[0], mc[1])
            yx, yc = delta_mixer(ax, ac, dn_w_in[j], dn_conv_w[j], dn_a_log[j], dn_dt_bias[j],
                                 dn_norm_g[j], dn_w_out[j], not last)
            hx = hx + mx[2] * yx
            if not last:
                hc = hc + mc[2] * yc
        hx = hx + mx[5] * peer(modulate(hx, norm2_g[i], mx[3], mx[4]),
                               peer_wq[i], peer_keys[i], peer_u[i], peer_v[i])
        if not last:
            hc = hc + mc[5] * peer(modulate(hc, norm2_g[i], mc[3], mc[4]),
                                   peer_wq[i], peer_keys[i], peer_u[i], peer_v[i])
    return rmsnorm(hx, final_g)


_drawn_inputs = setup_inputs


def setup_inputs(seed=0):
    import zlib

    import numpy as np

    out = dict(_drawn_inputs(seed))
    spreads = {}
    factors = {'ctx': 3.055,
     'c_ctx': 4.378,
     'norm1_g': 4.146,
     'norm2_g': 3.287,
     'dn_norm_g': 8.0,
     'final_g': 2.952}
    for name, (base, spread) in spreads.items():
        noise = np.random.default_rng([zlib.crc32(name.encode()), seed]).standard_normal(out[name].shape)
        drawn = base * np.exp(spread * noise) if base else spread * noise
        out[name] = __import__('jax').numpy.asarray(drawn.astype(out[name].dtype))
    for name, factor in factors.items():
        out[name] = (out[name] * factor).astype(out[name].dtype)
    return out
```

```python
from contextlib import ExitStack

import numpy as np
import concourse.bass as bass
import concourse.mybir as mybir

F32 = mybir.dt.float32
F32R = mybir.dt.float32r
BF16 = mybir.dt.bfloat16
U32 = mybir.dt.uint32
ACT = mybir.ActivationFunctionType
ALU = mybir.AluOpType
AX = mybir.AxisListType

P = 128
D = 1024
NC = D // P
T = 256
DEPTH = 2
GRID_W = 64
ROWS = T // GRID_W
EPS = 1e-6
WINDOWS = (2, 4, 8, 16)
HEADS = 8
TOPK = 16
NKEYS = 128
NT = T // P
NQ = 2 * HEADS
NE = NKEYS
NMOD = 6 * NC
GRP = 512
N_GRP = 6 * D // GRP
NIN = 4 * NC
OCTET, QUAD = 8, 4
N_OCT = T // OCTET
ACT_GATED = 5
RING = 4
AHEAD = 2

L0 = NQ + 2 * NE
W_IN = L0
W_OUT = L0 + NIN
L1 = L0 + NIN + NC
NBLOCKS = L1 + L0

PAIRS = [TOPK // (a + 1) for a in range(TOPK)]
OFF = [sum(PAIRS[:a]) for a in range(TOPK)]
NCAND = sum(PAIRS)
TAIL = next(a for a in range(TOPK) if PAIRS[a] == 1)


def build(nc, a, out):
    ctx = ExitStack()
    with ctx:
        def sb(name, shape, dt=F32):
            return ctx.enter_context(nc.sbuf_tensor(name, shape, dt))

        def sem(name):
            return ctx.enter_context(nc.semaphore(name))

        buf = sb("buf", [P, NE, T])
        h_hi = sb("h_hi", [P, NC, T], F32R)
        h_lo = sb("h_lo", [P, NC, T], F32R)
        raw = [sb(f"raw{i}", [P, NC, P]) for i in range(RING)]
        hi = [sb(f"hi{i}", [P, NC, P], F32R) for i in range(RING)]
        lo = [sb(f"lo{i}", [P, NC, P], F32R) for i in range(RING)]
        mods = sb("mods", [P, DEPTH, NMOD, 2])
        ident = sb("ident", [P, P])
        iota = sb("iota", [P, P])
        eps = sb("eps", [P, 1])
        pmark = sb("pmark", [P, 1])
        table = sb("table", [P, 16])
        gated1 = sb("gated1", [P, 16, P])
        one = sb("one", [P, 1])
        eps_q = sb("eps_q", [P, 1])
        fin_g2 = sb("fin_g2", [P, NC])
        mark = sb("mark", [P, 16])
        gT = sb("gT", [P, T])
        g4 = [sb(f"g4_{i}", [P, NKEYS, 4]) for i in range(2)]
        i1T, i2T = (hi[RING - 1][:, 2 * i:2 * i + 2, :].rearrange("p a b -> p (a b)") for i in range(2))
        flat = buf[:, :, :].rearrange("p b t -> p (b t)")

        def region(block, shape, dt=F32):
            n = int(np.prod(shape))
            if dt == BF16:
                n //= 2
            v = flat[:, block * T:block * T + n]
            if dt != F32:
                v = v.bitcast(dt)
            names = "abc"[:len(shape)]
            if len(shape) > 1:
                v = v.rearrange(f"p ({' '.join(names)}) -> p {' '.join(names)}",
                                **{c: s for c, s in zip(names[1:], shape[1:])})
            return v

        def at(off, *shape):
            v = flat[:, off:off + int(np.prod(shape))]
            if len(shape) > 1:
                names = "abc"[:len(shape)]
                v = v.rearrange(f"p ({' '.join(names)}) -> p {' '.join(names)}",
                                **{c: s for c, s in zip(names[1:], shape[1:])})
            return v

        res = [region(0, (NC, T)), region(116, (NC, T))]
        sq = region(84, (NC, T))
        hn = region(92, (NC, T))
        nrm = region(100, (NC, T))
        inv_std = region(108, (T,))
        std = region(109, (T,))
        pooled = region(8, (NC, T))
        counts = region(16, (2 * NC, T))
        pool_w = region(32, (4 * 4, P))
        box = [region(40, (2, 512)), region(44, (2, 512))]
        small = region(48, (1024,))
        row = [region(52 + 2 * i, (GRP,))[0:2] for i in range(2)]
        conv_x = region(8, (3 * HEADS, T))
        zs = region(32, (HEADS, T))
        conv_c = region(40, (2 * HEADS, T))
        state = [at(14336 + 1024 * i, HEADS, P) for i in range(2)]
        masks = at(16384, 21, P)
        pads = [at(19456 + 264 * i, T + 4) for i in range(4)]
        cw = at(20512, 5, 3 * HEADS)
        w_ab = at(20640, NC, 4 * HEADS)
        ab_c = at(20896, 3, 4 * HEADS)
        glog = at(20992, 4, 4 * HEADS)
        gtmp = at(21120, 4, 4 * HEADS)
        gs = at(21248, 4 * HEADS)
        neg_c = at(21280, HEADS)
        ex = at(21288, 5, HEADS)
        ones32 = at(21328, 4 * HEADS)
        out_g = at(21360, 1)
        fin_gT = at(21368, NC)
        work = [at(21504 + 1024 * i, HEADS, P) for i in range(10)]
        kT, X, BE, E, ET, K_t, KG, V_t, WT, U_t = work
        o_acc = region(40, (HEADS, T))
        AE = at(12288, HEADS, P)
        QG = at(13312, HEADS, P)
        M_CUM, M_CHUNK, M_SEG, M_STRICT, M_INCL, M_LEV = 0, 2, 3, 5, 7, 9

        keys = region(80, (NQ, NKEYS))
        rt = region(88, (1024,))
        top = [region(92 + q, (16, TOPK)) for q in range(4)]
        qT = region(96, (NQ, T))
        sc = region(112, (2 * HEADS, 2, NKEYS))

        pY = ctx.enter_context(nc.psum_tensor("pY", [P, 4, 512], F32))
        pS = [ctx.enter_context(nc.psum_tensor(f"pS{i}", [P, 512], F32)) for i in range(2)]
        pG = [ctx.enter_context(nc.psum_tensor(f"pG{i}", [P, 512], F32)) for i in range(2)]
        inv_d = sb("inv_d", [P, 1])
        ones_mean = inv_d[:, :].to_broadcast([P, P])

        raw_in = [sem(f"raw_in{i}") for i in range(RING)]
        hi_ready = sem("hi_ready")
        lo_ready = sem("lo_ready")
        block_done = sem("block_done")
        evacuated = sem("evacuated")
        s_done = sem("s_done")
        consts_in = sem("consts_in")
        ready = sem("ready")
        act_in = sem("act_in")
        silu_done = sem("silu_done")
        mod_in = [sem(f"mod_in{i}") for i in range(RING)]
        mod_done = sem("mod_done")
        row_ready = sem("row_ready")
        mods_T = sem("mods_T")
        mod_read = sem("mod_read")
        mod_ready = sem("mod_ready")
        dve = sem("dve")
        acts = sem("acts")
        squares = sem("squares")
        mean_sq = sem("mean_sq")
        std_ready = sem("std_ready")
        normed = sem("normed")
        pool_in = sem("pool_in")
        pooled_ready = sem("pooled_ready")
        pool_mm = sem("pool_mm")
        res_ready = sem("res_ready")
        h_split = sem("h_split")
        h_hi_ready = sem("h_hi_ready")
        spilled = sem("spilled")
        keys_in = sem("keys_in")
        q_ready = sem("q_ready")
        scores_done = sem("scores_done")
        scores_read = sem("scores_read")
        exp_in = sem("exp_in")
        exp_done = sem("exp_done")
        picks_ready = sem("picks_ready")
        picksT = sem("picksT")
        first_ready = sem("first_ready")
        rows_gated = sem("rows_gated")
        onehot = sem("onehot")
        gates_mm = sem("gates_mm")
        gates_sb = sem("gates_sb")
        gated = sem("gated")
        w_hi = sem("w_hi")
        w_lo = sem("w_lo")
        y_done = sem("y_done")
        res_in = sem("res_in")
        h_in = sem("h_in")
        out_done = sem("out_done")
        fin_ready = sem("fin_ready")

        def first_rows(o):
            return h_lo[:, 4 * (o % 2):4 * (o % 2) + 4, :].rearrange("p c (t k) -> p (c t) k", k=P)

        def second_rows(o):
            return h_hi[:, 4 * (o % 2):4 * (o % 2) + 4, :].rearrange("p c (t k) -> p (c t) k", k=P)

        def mod_slot(j):
            return raw[j][:, :, :].rearrange("p c e -> p (c e)").rearrange("p (c e) -> p c e", c=2)

        picks = [g4[i // 2][:, :, :].rearrange("p b t -> p (b t)")[:, (i % 2) * T:(i % 2 + 1) * T] for i in range(3)]
        U_ROUTE = RING * 2 * HEADS
        NEG = -3.0e38

        if True:
            (consts2_in, c_in, ab_mm, conv_done, silu_c, l2_sq, l2_mm, l2_std, l2_done, gl_x, gl_e, gl_done,
             staged, small_mm, trans_mm, kk_mm, expin, ex_ready, kv_sb, kvb, rb_mm, r_mm, be1, be2, ae1, ae2, er,
             b_ready, kq_mm, att, bt_mm, e0, rp, x_ready, e_mm, e_sb, wu_mm, wt_sb, u_sb, ws_mm, vn, ds_mm, s_upd,
             o_sq, o_mm, o_std, o_norm, y_res, evac_z) = (sem(n) for n in (
             "consts2_in c_in ab_mm conv_done silu_c l2_sq l2_mm l2_std l2_done gl_x gl_e gl_done "
             "staged small_mm trans_mm kk_mm expin ex_ready kv_sb kvb rb_mm r_mm be1 be2 ae1 ae2 er "
             "b_ready kq_mm att bt_mm e0 rp x_ready e_mm e_sb wu_mm wt_sb u_sb ws_mm vn ds_mm s_upd "
             "o_sq o_mm o_std o_norm y_res evac_z").split())

        block = ctx.enter_context(nc.Block())

        KD = 2 * L0
        NKV = 2 * HEADS
        K2 = KD + NKV + NIN + NC
        E2 = 2 * (NQ + NE)
        E3 = E2 + NKV + NIN + NC

        class Chain:
            def __init__(self, eng, s):
                self.eng, self.s, self.n, self.base = eng, s, 0, None

            def loop(self, i, per):
                self.base, self.i, self.per, self.start = self.n, i, per, self.n

            def end(self, trips):
                assert self.n - self.base == self.per, (self.n - self.base, self.per)
                self.n, self.base = self.base + self.per * trips, None

            def link(self, ins):
                self.mark(ins)
                self.wait()

            def mark(self, ins):
                self.n += 1
                ins.then_inc(self.s, 1)

            def wait(self):
                self.eng.wait_ge(self.s, self.n if self.base is None else self.i * self.per + self.n)

        @block.sync
        def _(sp):
            for v, (dst, src) in enumerate([(ident[:, :], a["ident"]), (small[:, 0:2 * NC], a["cT"]),
                                            (small[:, 16:16 + DEPTH * NMOD], a["mod_bT"]),
                                            (small[:, 112:112 + 2 * DEPTH * NC], a["gainT"]),
                                            (small[:, 144:144 + NC], a["pool_scaleT"]),
                                            (res[0], a["xT"]), (res[1], a["ctxT"]),
                                            (counts, a["counts"]), (pool_w, a["pool_wT"])]):
                sp.dma_start(dst, src).then_inc(consts_in, 16)

            with sp.Fori(0, DEPTH * N_GRP) as n:
                for j in range(RING):
                    sp.wait_ge(mod_done, RING * n + j + 1)
                    sp.dma_start(mod_slot(j), a["mod_wT"][bass.ds(RING * n + j, 1)]
                                 .rearrange("o p c e -> p (o c) e")).then_inc(mod_in[j], 16)

            def stream(k0, d0, n_blocks):
                with sp.Fori(0, n_blocks // RING) as n:
                    for j in range(RING):
                        sp.wait_ge(lo_ready, RING * n + (k0 + j + 1))
                        sp.dma_start(raw[j][:, :, :], a["blocks"][bass.ds(RING * n + (d0 + j), 1)]
                                     .rearrange("o p c e -> p (o c) e")).then_inc(raw_in[j], 16)

            sp.wait_ge(mod_done, RING + DEPTH * RING * N_GRP)
            stream(0, 0, L0)
            stream(L0, 0, L0)
            stream(KD, W_IN + HEADS, NKV)
            stream(KD + NKV, W_IN, NIN)
            stream(KD + NKV + NIN, W_OUT, NC)
            stream(K2, L1, L0)

        @block.scalar
        def _(act):
            s = nc.scalar
            tables = [0]

            def preload(func):
                s.activation(table[:, tables[0]:tables[0] + 1], eps[:, :], func)
                tables[0] += 1

            act.wait_ge(consts_in, 16 * 9)
            s.activation(small[:, 160:160 + 2 * NC], small[:, 0:2 * NC], ACT.Silu).then_inc(silu_done, 1)

            def norm(k, x, wait):
                wait()
                s.activation(sq, x, ACT.Square).then_inc(squares, 1)
                act.wait_ge(mean_sq, k + 1)
                if k:
                    act.wait_ge(normed, k)
                s.activation(std, pG[0][:, 0:T], ACT.Sqrt, bias=eps[:, :]).then_inc(std_ready, 1)

            def split_hi(n, k0, j):
                k = RING * n + (k0 + j) if n is not None else k0 + j
                slot = (k0 + j) % RING
                rounds = (k0 + j) // RING + 1
                act.wait_ge(raw_in[slot], (n + rounds) * 16 if n is not None else 16 * rounds)
                act.wait_ge(block_done, k + 1)
                s.copy(hi[slot][:, :, :], raw[slot][:, :, :]).then_inc(hi_ready, 1)

            def h_high(n_normed):
                act.wait_ge(normed, n_normed)
                s.copy(h_hi[:, :, :], nrm).then_inc(h_hi_ready, 1)

            def peer(g, k0, e0, last):
                preload(ACT.Gelu)
                with act.Fori(0, NQ // RING) as n:
                    for j in range(RING):
                        split_hi(n, k0, j + AHEAD)
                        act.wait_ge(block_done, RING * n + (k0 + j + 1 + RING))
                        s.copy(qT[:, bass.ds(RING * n + j, 1), :], pS[j % 2][:, 0:T].unsqueeze(1)).then_inc(evacuated, 1)
                def u_blocks(b0, nb):
                    with act.Fori(0, nb // RING) as n:
                        for j in range(RING):
                            split_hi(n, k0 + NQ + b0, j + AHEAD)
                            act.wait_ge(block_done, RING * n + (k0 + NQ + b0 + j + 1 + RING))
                            s.activation(buf[:, bass.ds(RING * n + (b0 + j), 1), :], pS[j % 2][:, 0:T].unsqueeze(1), ACT.Gelu).then_inc(evacuated, 1)
                act.wait_ge(spilled, (48, 64, 80)[g])
                u_blocks(0, U_ROUTE)
                act.wait_ge(exp_in, g + 1)
                s.activation(top[0], top[0], ACT.Exp).then_inc(exp_done, 1)
                preload(ACT.Gelu)
                u_blocks(U_ROUTE, NE - U_ROUTE)
                def gate_rows(n, o):
                    act.wait_ge(first_ready, 2 * n + (N_OCT * g + o + 1) if n is not None else N_OCT * g + o + 1)
                    for t in range(ACT_GATED):
                        tok = 16 * n + (8 * o + t) if n is not None else 8 * o + t
                        i = s.activation(gated1[:, 8 * (o % 2) + t, :], first_rows(o)[:, t, :].bitcast(F32), ACT.Copy, scale=gT[:, bass.ds(tok, 1)])
                        if t in (QUAD - 1, ACT_GATED - 1):
                            i.then_inc(rows_gated, 1)

                def gates_out(n, o):
                    for q in range(2):
                        k = 2 * o + q
                        act.wait_ge(gates_mm, 4 * n + (2 * N_OCT * g + k + 5) if n is not None else 2 * N_OCT * g + k + 5)
                        act.wait_ge(gated, 4 * n + (2 * N_OCT * g + k + 1) if n is not None else 2 * N_OCT * g + k + 1)
                        s.copy(g4[q][:, :, :], pG[q][:, :].rearrange("p (t b) -> p b t", t=QUAD)).then_inc(gates_sb, 1)

                gate_rows(None, 0)
                with act.Fori(0, N_OCT // 2 - 1) as n:
                    for o in range(2):
                        gate_rows(n, o + 1)
                        gates_out(n, o)
                gate_rows(None, N_OCT - 1)
                gates_out(None, N_OCT - 2)
                gates_out(None, N_OCT - 1)
                kv = k0 + NQ + NE
                act.wait_ge(gated, 2 + 64 * (g + 1))
                def v_body(n, b0, peel):
                    for j in range(RING):
                        b = RING * n + (b0 + j) if n is not None else b0 + j
                        act.wait_ge(block_done, b + (kv + 1))
                        s.copy(w_h(j), buf[:, bass.ds(b, 1), :] if n is not None else buf[:, b:b + 1, :]).then_inc(w_hi, 1)
                        if not (peel and j + AHEAD >= RING):
                            split_hi(n, kv + b0, j + AHEAD)
                nl = NE // RING - (1 if last else 0)
                with act.Fori(0, nl) as n:
                    v_body(n, 0, False)
                if last:
                    v_body(None, NE - RING, True)

            def w_h(j):
                return h_hi[:, j:j + 1, :]

            def init():
                for j in range(AHEAD):
                    split_hi(None, 0, j)

            def adaln(L, g0, groups):
                with act.Fori(0, groups // 2) as n:
                    for i in range(2):
                        m = 2 * n + (L * N_GRP + g0 + i)
                        act.wait_ge(mod_done, m * RING + 2 * RING)
                        s.copy(row[i], pS[i][0:2, :]).then_inc(row_ready, 1)

            adaln(0, 0, N_GRP)
            for k in range(2):
                norm(2 * k, res[k], lambda: act.wait_ge(mod_ready, 1))
                adaln(1, k * N_GRP // 2, N_GRP // 2)
                norm(2 * k + 1, res[k], lambda: act.wait_ge(res_ready, k + 1))
            h_high(4)
            init()
            peer(0, 0, 0, False)
            act.wait_ge(h_in, 16)
            s.copy(h_hi[:, :, :], hn).then_inc(h_hi_ready, 1)
            peer(1, L0, NQ + NE, False)

            ACTS = [0]

            def s_evac(k0, e0, nb, f):
                with act.Fori(0, nb // RING) as n:
                    for j in range(RING):
                        split_hi(n, k0, j + AHEAD)
                        act.wait_ge(block_done, RING * n + (k0 + j + 1 + RING))
                        f(n, j)

            def to_pads(c0):
                def f(n, j):
                    act.wait_ge(conv_done, RING * n + (c0 + j + 1))
                    s.copy(pads[j][:, 2:2 + T], pS[j % 2][:, 0:T]).then_inc(evacuated, 1)
                return f

            def to_z(n, j):
                s.activation(zs[:, bass.ds(RING * n + j, 1), :], pS[j % 2][:, 0:T].unsqueeze(1), ACT.Silu).then_inc(evacuated, 1)

            norm(4, res[1], lambda: act.wait_ge(c_in, 16))
            h_high(5)
            s_evac(KD, E2, NKV, to_pads(0))
            act.wait_ge(conv_done, RING + NKV)
            s.activation(conv_c, conv_c, ACT.Silu).then_inc(silu_c, 1)
            norm(5, res[0], lambda: act.wait_ge(fin_ready, 2))
            h_high(6)
            s_evac(KD + NKV, E2 + NKV, 3 * HEADS, to_pads(NKV))
            act.wait_ge(conv_done, RING + NKV + 3 * HEADS)
            s.activation(conv_x, conv_x, ACT.Silu).then_inc(silu_c, 1)
            s_evac(KD + NKV + 3 * HEADS, E2 + NKV + 3 * HEADS, HEADS, to_z)
            act.wait_ge(silu_c, 2)
            for r, x in enumerate((conv_c[:, 0:HEADS], conv_x[:, 0:HEADS], conv_x[:, HEADS:2 * HEADS])):
                if r:
                    act.wait_ge(l2_mm, r)
                s.activation(sq, x, ACT.Square).then_inc(l2_sq, 1)
                act.wait_ge(l2_mm, r + 1)
                if r:
                    act.wait_ge(l2_done, r)
                q_scale = float(P) if r == 1 else 1.0
                s.activation(hn.rearrange("p c t -> p (c t)"), pY[:, :, :].rearrange("p a b -> p (a b)"), ACT.Sqrt,
                             bias=(eps_q if r == 1 else eps)[:, :], scale=D * q_scale).then_inc(l2_std, 1)
            act.wait_ge(consts2_in, 16 * 7)
            act.wait_ge(gl_x, 1)
            s.activation(ab_c[:, 2], ab_c[:, 2], ACT.Exp).then_inc(gl_e, 1)
            s.activation(gtmp, gtmp, ACT.Exp).then_inc(gl_e, 1)
            act.wait_ge(gl_e, 2)
            s.activation(gtmp, gtmp, ACT.Ln, bias=one[:, :]).then_inc(gl_e, 1)

            def scan_body(ph, it, d):
                n = 4 * ph + d
                tile = it if d == 0 else it * -1 + 1
                kx, vx = (conv_c[:, 0:HEADS], conv_c[:, HEADS:]) if ph == 0 else (conv_x[:, HEADS:2 * HEADS], conv_x[:, 2 * HEADS:])
                act.wait_ge(s_upd, 4 * it + (2 * n + 1))
                cols = bass.ds(tile * P, P)
                s.copy(kT, kx[:, :, cols])
                s.copy(X, vx[:, :, cols])
                s.copy(gs.unsqueeze(1), glog[:, bass.ds(tile + 2 * ph, 1), :]).then_inc(staged, 1)
                act.wait_ge(expin, 2 * it + (n + 1))
                s.activation(ex, ex, ACT.Exp).then_inc(ex_ready, 1)
                act.wait_ge(trans_mm, 2 * it + (n + 1))
                pyf = pY[:, :, :].rearrange("p a (b c) -> p (a b) c", c=P)
                s.copy(K_t, pyf[:, 0:HEADS, :])
                s.copy(V_t, pyf[:, HEADS:, :]).then_inc(kv_sb, 1)
                act.wait_ge(be1, 2 * it + (n + 1))
                for h in range(HEADS):
                    i = s.activation(BE[:, h, :], BE[:, h, :], ACT.Exp, bias=neg_c[:, h:h + 1])
                i.then_inc(be2, 1)
                if ph:
                    act.wait_ge(ae1, 2 * it + d + 1)
                    s.activation(QG, pyf[:, HEADS:, :], ACT.Exp).then_inc(er, 1)
                    for h in range(HEADS):
                        i = s.activation(AE[:, h, :], AE[:, h, :], ACT.Exp, bias=neg_c[:, h:h + 1])
                    i.then_inc(ae2, 1)
                for lv in range(5):
                    for q in range(2):
                        act.wait_ge(e_mm, 20 * it + (10 * n + 2 * lv + q + 1))
                        if lv < 4:
                            s.copy(E[:, 4 * q:4 * q + 4, :], pyf[:, 4 * q:4 * q + 4, :])
                            s.copy(ET[:, 4 * q:4 * q + 4, :], pyf[:, 8 + 4 * q:12 + 4 * q, :]).then_inc(e_sb, 1)
                        else:
                            s.copy(E[:, 4 * q:4 * q + 4, :], pyf[:, 4 * q:4 * q + 4, :]).then_inc(e_sb, 1)
                act.wait_ge(wu_mm, 2 * it + (n + 1))
                s.copy(WT, pyf[:, 0:HEADS, :]).then_inc(wt_sb, 1)

            act.wait_ge(gl_done, 1)
            act.wait_ge(l2_done, 3)
            preload(ACT.Exp)
            for ph in range(2):
                with act.Fori(0, 2) as it:
                    for d in range(2):
                        scan_body(ph, it, d)
            act.wait_ge(s_upd, 17)
            s.activation(sq, o_acc, ACT.Square).then_inc(o_sq, 1)
            act.wait_ge(o_mm, 1)
            s.activation(hn.rearrange("p c t -> p (c t)"), pY[:, :, :].rearrange("p a b -> p (a b)"), ACT.Sqrt,
                         bias=eps[:, :], scale=float(NC)).then_inc(o_std, 1)
            act.wait_ge(o_norm, 1)
            s.copy(h_hi[:, :, :], o_acc).then_inc(h_hi_ready, 1)
            with act.Fori(0, NC // RING) as n:
                for j in range(RING):
                    split_hi(n, KD + NKV + NIN, j + AHEAD)
            norm(6, res[0], lambda: act.wait_ge(y_res, NC))
            h_high(7)
            peer(2, K2, E3, True)
            act.wait_ge(fin_ready, 3)
            norm(7, res[0], lambda: None)

        @block.vector
        def _(ve):
            v = nc.vector
            ch = Chain(ve, dve)
            link = ch.link
            v.memset(eps[:, :], EPS).then_inc(ready, 1)
            v.memset(inv_d[:, :], 1.0 / D).then_inc(ready, 1)
            v.memset(mark[:, 12:13], 0.0).then_inc(gates_sb, 2)
            v.memset(mark[:, 13:14], 0.0).then_inc(lo_ready, RING)

            ve.wait_ge(consts_in, 16 * 9)
            def adaln(L):
                ve.wait_ge(mods_T, N_GRP * (L + 1))
                m = mods[:, L]
                bias = small[:, 16 + L * NMOD:16 + (L + 1) * NMOD]
                link(v.tensor_tensor(m, pG[L][:, 0:2 * NMOD].rearrange("p (a b) -> p a b", b=2),
                                     bias.unsqueeze(2).to_broadcast([P, NMOD, 2]), ALU.add))
                for sub in range(2):
                    g = small[:, 112 + (2 * L + sub) * NC:112 + (2 * L + sub + 1) * NC]
                    scale = m[:, (3 * sub + 1) * NC:(3 * sub + 2) * NC]
                    link(v.tensor_scalar(scale, scale, 1.0, None, ALU.add))
                    link(v.tensor_tensor(scale, scale, g.unsqueeze(2).to_broadcast([P, NC, 2]), ALU.mult))
                if L == 0:
                    gate = m[:, 2 * NC:3 * NC]
                    link(v.tensor_tensor(gate, gate, small[:, 144:144 + NC].unsqueeze(2).to_broadcast([P, NC, 2]), ALU.mult))
                v.memset(mark[:, 2 + 8 * L:3 + 8 * L], 0.0).then_inc(mod_ready, 1)

            adaln(0)

            def norm(k, x, layer, sub, which):
                ve.wait_ge(std_ready, k + 1)
                link(v.reciprocal(inv_std, std))
                link(v.tensor_tensor(hn, x, inv_std.unsqueeze(1).to_broadcast([P, NC, T]), ALU.mult))
                for c in range(NC):
                    ins = v.tensor_scalar(nrm[:, c, :], hn[:, c, :], mods[:, layer, (3 * sub + 1) * NC + c, which:which + 1],
                                          mods[:, layer, 3 * sub * NC + c, which:which + 1], ALU.mult, ALU.add)
                ins.then_inc(normed, 1)

            def box_add(dst, x, y):
                link(v.tensor_tensor(dst, x, y, ALU.add))

            def pool_grid():
                for g, w in enumerate(WINDOWS):
                    x = nrm[:, 2 * g:2 * g + 2, :]
                    xr = x.rearrange("p c (r w) -> p c r w", r=ROWS)
                    A, B = (t_[:, :, :].rearrange("p c n -> p (c n)")[:, 0:2 * ROWS * 96]
                            .rearrange("p (c r w) -> p c r w", c=2, r=ROWS) for t_ in box_big)
                    link(v.memset(box_big[0][:, :, :], 0.0))
                    link(v.memset(box_big[1][:, :, :], 0.0))
                    mid = slice(16, 16 + GRID_W)
                    if w == 2:
                        v.tensor_copy(A[:, :, 0:1, mid], xr[:, :, 0:1, :])
                        for cc in range(2):
                            i = v.tensor_tensor(A[:, cc, 1:ROWS, mid], xr[:, cc, 1:ROWS, :], xr[:, cc, 0:ROWS - 1, :], ALU.add)
                        link(i)
                    elif w == 4:
                        for cc in range(2):
                            i = v.tensor_tensor(B[:, cc, 0:ROWS - 1, mid], xr[:, cc, 0:ROWS - 1, :], xr[:, cc, 1:ROWS, :], ALU.add)
                        link(i)
                        for cc in range(2):
                            v.tensor_copy(A[:, cc, 0:1, mid], B[:, cc, 0:1, mid])
                            v.tensor_tensor(A[:, cc, 1:2, mid], B[:, cc, 1:2, mid], xr[:, cc, 0:1, :], ALU.add)
                            v.tensor_tensor(A[:, cc, 2:3, mid], B[:, cc, 2:3, mid], B[:, cc, 0:1, mid], ALU.add)
                            i = v.tensor_tensor(A[:, cc, 3:4, mid], B[:, cc, 1:2, mid], xr[:, cc, 3:4, :], ALU.add)
                        link(i)
                    else:
                        for cc in range(2):
                            i = v.tensor_tensor(B[:, cc, 0:2, mid], xr[:, cc, 0:2, :], xr[:, cc, 2:4, :], ALU.add)
                        link(i)
                        for cc in range(2):
                            i = v.tensor_tensor(A[:, cc, 0:1, mid], B[:, cc, 0:1, mid], B[:, cc, 1:2, mid], ALU.add)
                        link(i)
                        for cc in range(2):
                            i = v.tensor_copy(A[:, cc, 1:ROWS, mid], A[:, cc, 0:1, mid].to_broadcast([P, ROWS - 1, GRID_W]))
                        link(i)
                    A2, B2 = (t_.rearrange("p c r w -> p (c r) w") for t_ in (A, B))
                    if w != 2:
                        link(v.memset(box_big[1][:, :, :], 0.0))
                    line_windows(A2, B2, w, GRID_W, pooled[:, 2 * g:2 * g + 2, :].rearrange("p c (r w) -> p (c r) w", r=ROWS))
                    finish_pool(0, g, x)

            def line_windows(A, B, w, n, out):
                lo_, hi_ = 16 - w, 16 + n + w - 1
                src, dst = A, B
                step = 1
                first = True
                width = 2
                while width <= w:
                    r = w // 2 - width // 2
                    lo_, hi_ = 16 - r, 16 + n + r
                    if first:
                        x0, x1 = src[:, :, lo_ - 1:hi_ - 1], src[:, :, lo_:hi_]
                        first = False
                    else:
                        q = width // 4
                        x0, x1 = src[:, :, lo_ - q:hi_ - q], src[:, :, lo_ + q:hi_ + q]
                    if width == w:
                        link(v.tensor_tensor(out, x0, x1, ALU.add))
                    else:
                        link(v.tensor_tensor(dst[:, :, lo_:hi_], x0, x1, ALU.add))
                    src, dst = dst, src
                    width *= 2

            def finish_pool(which, g, x):
                o = pooled[:, 2 * g:2 * g + 2, :]
                link(v.tensor_tensor(o, o, counts[:, which * NC + 2 * g:which * NC + 2 * g + 2, :], ALU.mult))
                link(v.tensor_tensor(o, o, x, ALU.subtract))

            def pool_line():
                for g, w in enumerate(WINDOWS):
                    x = nrm[:, 2 * g:2 * g + 2, :]
                    A, B = (t_[:, :, 0:T + 32] for t_ in box_big)
                    link(v.memset(box_big[0][:, :, :], 0.0))
                    link(v.memset(box_big[1][:, :, :], 0.0))
                    link(v.tensor_copy(A[:, :, 16:16 + T], x))
                    line_windows(A, B, w, T, pooled[:, 2 * g:2 * g + 2, :])
                    finish_pool(1, g, x)

            box_big = box

            def add_branch(k, x, ps_of, layer, sec, which, signal):
                for c in range(NC):
                    i = v.scalar_tensor_tensor(x[:, c, :], ps_of(c), mods[:, layer, sec * NC + c, which:which + 1],
                                               x[:, c, :], ALU.mult, ALU.add)
                i.then_inc(signal, 1)

            def y_chunk(c):
                return pY[:, c // 2, (c % 2) * T:(c % 2) * T + T]

            for k in range(2):
                norm(2 * k, res[k], 0, 0, k)
                ve.wait_ge(normed, 2 * k + 1)
                (pool_grid if k == 0 else pool_line)()
                v.memset(mark[:, 3:4], 0.0).then_inc(pooled_ready, 1)
                ve.wait_ge(pool_mm, k + 1)
                add_branch(k, res[k], y_chunk, 0, 2, k, res_ready)
                ve.wait_ge(res_ready, k + 1)
                norm(2 * k + 1, res[k], 0, 1, k)
                if k == 0:
                    ve.wait_ge(spilled, 32)

            def split_lo(n, k0, j):
                k = RING * n + (k0 + j) if n is not None else k0 + j
                slot = (k0 + j) % RING
                ve.wait_ge(hi_ready, k + 1)
                v.tensor_tensor(lo[slot][:, :, :], raw[slot][:, :, :], hi[slot][:, :, :].bitcast(F32), ALU.subtract).then_inc(lo_ready, 1)

            def link_max(ins):
                link(ins)
                v.memset(mark[:, 0:1], 0.0)

            def route_unit(u, n):
                s2 = u[:, 0:256]
                s2b = u[:, 256:384]
                val = u[:, 384:416]
                cand = u[:, 416:466]
                candb = u[:, 480:530]
                best = u[:, 544:560]
                idx = u[:, 576:624].bitcast(U32)
                link_max(v.tensor_copy(s2, sc.rearrange("p u h k -> p u (h k)")[:, bass.ds(n, 1), :].rearrange("p o k -> p (o k)")))
                for hf in range(2):
                    x = s2[:, hf * NKEYS:(hf + 1) * NKEYS]
                    a0, a1 = val[:, 16 * hf:16 * hf + 8], val[:, 16 * hf + 8:16 * hf + 16]
                    link_max(v.max(a0, x))
                    v.max_index(idx[:, 16 * hf:16 * hf + 8], a0, x)
                    link_max(v.match_replace(s2b, a0, x, NEG))
                    link_max(v.max(a1, s2b))
                    v.max_index(idx[:, 16 * hf + 8:16 * hf + 16], a1, s2b)
                for aa in range(TAIL):
                    v.tensor_scalar(cand[:, OFF[aa]:OFF[aa] + PAIRS[aa]], val[:, 16:16 + PAIRS[aa]], val[:, aa:aa + 1], None, ALU.add)
                link_max(v.tensor_scalar(cand[:, OFF[TAIL]:NCAND], val[:, TAIL:TOPK], val[:, 16:17], None, ALU.add))
                a0, a1 = best[:, 0:8], best[:, 8:16]
                link_max(v.max(a0, cand))
                v.max_index(idx[:, 32:40], a0, cand)
                link_max(v.match_replace(candb, a0, cand, NEG))
                link_max(v.max(a1, candb))
                link(v.max_index(idx[:, 40:48], a1, candb))
                v.tensor_copy(top[0][:, bass.ds(n, 1), :], best.unsqueeze(1))
                for q_, src in ((2, 0), (3, 16), (1, 32)):
                    last = v.tensor_copy(top[q_][:, bass.ds(n, 1), :], idx[:, src:src + 16].unsqueeze(1))
                link(last)
            UNIT_LINKS = 1 + 2 * 3 + 1 + 3 + 1 + 1

            def peer(g, k0, e0, last):
                kq, ku = k0, k0 + NQ
                with ve.Fori(0, NQ // RING) as n:
                    for j in range(RING):
                        split_lo(n, kq, j + AHEAD)
                if g == 1:
                    ve.wait_ge(spilled, 64)
                for r in range(NT):
                    ve.wait_ge(scores_done, NT * g + r + 1)
                    i = v.tensor_copy(sc[:, 8 * r:8 * r + 8].rearrange("p u h k -> p (u h k)"),
                                      pY[:, :, :].rearrange("p a b -> p (a b)"))
                    i.then_inc(scores_read, 1)
                ve.wait_ge(scores_read, NT * g + NT)
                with ve.Fori(0, 2 * HEADS) as n:
                    ch.loop(n, UNIT_LINKS)
                    for j in range(RING):
                        split_lo(n, ku, j + AHEAD)
                        if j == 1:
                            route_unit(rt, n)
                    ch.end(2 * HEADS)
                b = RING * 2 * HEADS
                steps = post_steps()
                v0 = [b]
                def blocks(nb):
                    with ve.Fori(0, nb // RING) as n:
                        for j in range(RING):
                            split_lo(n, ku + v0[0], j + AHEAD)
                    v0[0] += nb
                for st in steps:
                    st(g)
                    blocks(RING)
                assert v0[0] <= 88, v0[0]
                blocks(NE - v0[0])
                ve.wait_ge(picksT, g + 1)
                v.tensor_copy(gT[:, :], pG[1][:, 0:T])
                v.tensor_copy(i1T, pG[0][:, 0:T])
                link(v.tensor_copy(i2T, pG[0][:, T:2 * T]))
                v.memset(mark[:, 4:5], 0.0)
                with ve.Fori(0, N_OCT // 2) as n:
                    for o in range(2):
                        ve.wait_ge(gates_mm, 4 * n + (2 * N_OCT * g + 2 * o + 2))
                        def onehot_rows(dst, idx, m):
                            return v.tensor_tensor(dst[:, 0:m, :], iota[:, :].unsqueeze(1).to_broadcast([P, m, P]),
                                                   idx[:, bass.ds(16 * n + 8 * o, m)].bitcast(F32).unsqueeze(2).to_broadcast([P, m, P]), ALU.is_equal)
                        onehot_rows(first_rows(o), i1T, ACT_GATED).then_inc(first_ready, 1)
                        onehot_rows(second_rows(o), i2T, OCTET).then_inc(onehot, 1)
                        for t in range(ACT_GATED, OCTET):
                            tok = 16 * n + (8 * o + t)
                            i = v.tensor_scalar(gated1[:, 8 * o + t, :], iota[:, :], i1T[:, bass.ds(tok, 1)].bitcast(F32), gT[:, bass.ds(tok, 1)], ALU.is_equal, ALU.mult)
                        i.then_inc(onehot, 1)
                kv = k0 + NQ + NE
                def v_body(n, b0, peel):
                    for j in range(RING):
                        b = RING * n + (b0 + j) if n is not None else b0 + j
                        ve.wait_ge(w_hi, b + (NE * g + 1))
                        v.tensor_tensor(h_lo[:, j:j + 1, :], buf[:, bass.ds(b, 1), :] if n is not None else buf[:, b:b + 1, :],
                                        h_hi[:, j:j + 1, :].bitcast(F32), ALU.subtract).then_inc(w_lo, 1)
                        if not (peel and j + AHEAD >= RING):
                            split_lo(n, kv + b0, j + AHEAD)
                nl = NE // RING - (1 if last else 0)
                with ve.Fori(0, nl) as n:
                    v_body(n, 0, False)
                if last:
                    v_body(None, NE - RING, True)

            def post_steps():
                A_ = rt[:, 0:256]
                B_ = rt[:, 256:512]
                g16 = rt[:, 512:528]
                g16r = rt[:, 528:544]
                pos = top[1].rearrange("p u k -> p (u k)")
                val = top[0]
                hot = region(96, (HEADS, TOPK, TOPK))
                hotm = region(104, (HEADS, TOPK, TOPK))
                def softmax_in(g):
                    link(v.tensor_copy(g16, val[:, :, 0]))
                    v.tensor_tensor(val, val, g16.unsqueeze(2).to_broadcast([P, 16, TOPK]), ALU.subtract).then_inc(exp_in, 1)
                    link(v.tensor_scalar(A_, pos, -(OFF[TAIL] - 1.0), 0.0, ALU.add, ALU.max))
                    link(v.tensor_tensor(B_, pos, A_, ALU.subtract))
                def off_a(lo_, hi_):
                    def f(g):
                        for m in range(lo_, hi_):
                            if m < TAIL:
                                link(v.scalar_tensor_tensor(A_, pos, float(OFF[m]), A_, ALU.is_ge, ALU.add))
                            w = float(PAIRS[m - 1]) if m < TAIL else 1.0
                            link(v.tensor_scalar(rt[:, 544:800], pos, float(OFF[m]), w, ALU.is_ge, ALU.mult))
                            link(v.tensor_tensor(B_, B_, rt[:, 544:800], ALU.subtract))
                    return f
                def gather(which, tile, part):
                    pick = (A_ if which == 0 else B_)[:, tile * P:(tile + 1) * P]
                    lst = top[2 + which][:, tile * HEADS:(tile + 1) * HEADS, :]
                    dst = (gi1 if which == 0 else gi2)[:, tile * P:(tile + 1) * P]
                    io = iota[:, 0:TOPK]
                    def f(g):
                        if part == 0:
                            link(v.tensor_tensor(hot.rearrange("p h k a -> p (h k) a"), pick.unsqueeze(2).to_broadcast([P, P, TOPK]),
                                                 io.unsqueeze(1).to_broadcast([P, P, TOPK]), ALU.is_equal))
                            link(v.tensor_tensor(hotm, hot, lst.unsqueeze(2).to_broadcast([P, HEADS, TOPK, TOPK]), ALU.mult))
                        else:
                            link(v.tensor_reduce(dst.rearrange("p (h k) -> p h k", h=HEADS), hotm, AX.X, ALU.add))
                    return f
                gi1, gi2 = region(86, (256,)), region(87, (256,))
                def both(*fs):
                    def f(g):
                        for x in fs:
                            x(g)
                    return f
                def softmax_out(g):
                    ve.wait_ge(exp_done, g + 1)
                    link(v.tensor_reduce(g16, val, AX.X, ALU.add))
                    link(v.reciprocal(g16r, g16))
                    link(v.tensor_tensor(val, val, g16r.unsqueeze(2).to_broadcast([P, 16, TOPK]), ALU.mult))
                def done(g):
                    ve.wait_ge(gated, 2 + 64 * g)
                    v.tensor_copy(picks[0][:, :], gi1)
                    v.tensor_copy(picks[1][:, :], gi2)
                    v.tensor_copy(picks[2][:, :], val.rearrange("p u k -> p (u k)")).then_inc(picks_ready, 1)
                return [softmax_in, off_a(1, TAIL + 1), both(gather(0, 0, 0), gather(0, 0, 1)), both(gather(0, 1, 0), gather(0, 1, 1)),
                        both(gather(1, 0, 0), gather(1, 0, 1)), both(gather(1, 1, 0), gather(1, 1, 1), softmax_out, done)]

            def h_low(k, src):
                ve.wait_ge(h_hi_ready, k + 1)
                v.tensor_tensor(h_lo[:, :, :], src, h_hi[:, :, :].bitcast(F32), ALU.subtract).then_inc(h_split, 1)

            h_low(0, nrm)
            adaln(1)
            for j in range(AHEAD):
                split_lo(None, 0, j)
            peer(0, 0, 0, False)
            h_low(1, hn)
            ve.wait_ge(res_in, 16)
            add_branch(2, res[1], y_chunk, 0, 5, 1, fin_ready)
            peer(1, L0, NQ + NE, False)
            ve.wait_ge(block_done, RING + KD)
            ve.wait_ge(res_in, 32)
            add_branch(3, res[0], y_chunk, 0, 5, 0, fin_ready)

            def conv_section(k0, c0, w0, dst, nb):
                with ve.Fori(0, nb // RING) as n:
                    ch.loop(n, RING * 4)
                    for j in range(RING):
                        split_lo(n, k0, j + AHEAD)
                        ve.wait_ge(evacuated, RING * n + (c0 + E2 + j + 3))
                        o = dst[:, bass.ds(RING * n + j, 1), :].rearrange("p o t -> p (o t)")
                        tap = [cw[:, i, bass.ds(RING * n + (w0 + j), 1)] for i in range(5)]
                        link(v.tensor_scalar(o, pads[j][:, 0:T], tap[0], None, ALU.mult))
                        for i in range(1, 5):
                            ins = v.scalar_tensor_tensor(o, pads[j][:, i:i + T], tap[i], o, ALU.mult, ALU.add)
                            if i < 4:
                                link(ins)
                        ins.then_inc(conv_done, 1)
                    ch.end(nb // RING)

            norm(4, res[1], 1, 0, 1)
            h_low(2, nrm)
            ve.wait_ge(consts2_in, 16 * 7)
            v.memset(one[:, :], 1.0)
            v.memset(eps_q[:, :], EPS * P)
            for i in range(4):
                ins = v.memset(pads[i], 0.0)
            ins.then_inc(conv_done, RING)
            conv_section(KD, 0, HEADS, conv_c, NKV)
            ve.wait_ge(ab_mm, 1)
            norm(5, res[0], 1, 0, 0)
            h_low(3, nrm)
            conv_section(KD + NKV, NKV, 0, conv_x, 3 * HEADS)
            with ve.Fori(0, HEADS // RING) as n:
                for j in range(RING):
                    split_lo(n, KD + NKV + 3 * HEADS, j + AHEAD)
            for r, x in enumerate((conv_c[:, 0:HEADS], conv_x[:, 0:HEADS], conv_x[:, HEADS:2 * HEADS])):
                ve.wait_ge(l2_std, r + 1)
                link(v.reciprocal(hn, hn))
                v.tensor_tensor(x, x, hn, ALU.mult).then_inc(l2_done, 1)
            ve.wait_ge(ab_mm, 2)
            rows = lambda i: ab_c[:, i:i + 1, :].to_broadcast([P, 4, 4 * HEADS])
            link(v.tensor_tensor(glog, pG[1][:, 0:P].rearrange("p (a b) -> p a b", a=4), rows(0), ALU.mult))
            link(v.tensor_tensor(glog, glog, rows(1), ALU.add))
            v.scalar_tensor_tensor(gtmp, glog, -1.0, glog, ALU.mult, ALU.min).then_inc(gl_x, 1)
            ve.wait_ge(gl_x, 1)
            link(v.tensor_scalar(glog, glog, 0.0, None, ALU.max))
            ve.wait_ge(gl_e, 3)
            link(v.tensor_tensor(glog, glog, gtmp, ALU.add))
            link(v.tensor_tensor(glog, glog, rows(2), ALU.mult))
            link(v.tensor_scalar(glog, glog, -1.0, None, ALU.mult))
            v.memset(mark[:, 5:6], 0.0).then_inc(gl_done, 1)
            v.memset(state[0], 0.0)
            v.memset(state[1], 0.0).then_inc(s_upd, 1)

            gate1 = mods[:, 1, 2 * NC:3 * NC, 0]

            def mask(i):
                return masks[:, i:i + 1, :].to_broadcast([P, HEADS, P])

            def mask4(i):
                return masks[:, i:i + 1, :].to_broadcast([P, 4, P])

            eye = ident[:, :].unsqueeze(1)

            def scan_body(ph, it, d):
                n = 4 * ph + d
                one_ = 2 * it + (n + 1)
                tile = it if d == 0 else it * -1 + 1
                lb = gs[:, 16 * d + 8:16 * d + 16]
                pyf = pY[:, :, :].rearrange("p a (b c) -> p (a b) c", c=P)
                ve.wait_ge(s_upd, 4 * it + (2 * n + 1))
                ve.wait_ge(small_mm, one_)
                c_ = pG[0][:, 0:8]
                v.tensor_scalar(neg_c, c_, -1.0, None, ALU.mult)
                link(v.tensor_copy(ex[:, 1], c_))
                v.tensor_tensor(ex[:, 0], c_, lb, ALU.add)
                v.tensor_copy(ex[:, 2], lb)
                v.tensor_copy(ex[:, 3:5], pG[0][:, 16:32].rearrange("p (a b) -> p a b", a=2))
                v.tensor_tensor(ex[:, 1], pG[0][:, 8:16], ex[:, 1], ALU.subtract).then_inc(expin, 1)
                ve.wait_ge(rb_mm, one_)
                v.tensor_tensor(BE, pyf[:, 0:HEADS, :], mask(M_STRICT + d), ALU.add).then_inc(be1, 1)
                if ph:
                    ve.wait_ge(r_mm, 2 * it + d + 1)
                    v.tensor_tensor(AE, pyf[:, HEADS:, :], mask(M_INCL + d), ALU.add).then_inc(ae1, 1)
                ve.wait_ge(be2, one_)
                ve.wait_ge(kk_mm, one_)
                for q in range(2):
                    i = v.scalar_tensor_tensor(BE[:, 4 * q:4 * q + 4, :], pS[q][:, :].rearrange("p (a b) -> p a b", a=4), -1.0,
                                               BE[:, 4 * q:4 * q + 4, :], ALU.mult, ALU.mult)
                i.then_inc(b_ready, 1)
                ve.wait_ge(bt_mm, one_)
                ve.wait_ge(b_ready, one_)
                v.tensor_tensor(E, BE, mask(M_LEV + 1 - d), ALU.mult)
                link(v.tensor_tensor(ET, pyf[:, 0:HEADS, :], mask(M_LEV + d), ALU.mult))
                v.tensor_tensor(E, E, eye.to_broadcast([P, HEADS, P]), ALU.add)
                v.tensor_tensor(ET, ET, eye.to_broadcast([P, HEADS, P]), ALU.add).then_inc(e0, 1)
                if ph:
                    cols = bass.ds(tile * P, P)
                    ve.wait_ge(er, 2 * it + d + 1)
                    v.tensor_tensor(QG, QG, conv_x[:, 0:HEADS, cols], ALU.mult)
                    ve.wait_ge(ae2, 2 * it + d + 1)
                    ve.wait_ge(kq_mm, 2 * it + d + 1)
                    for q in range(2):
                        i = v.tensor_tensor(AE[:, 4 * q:4 * q + 4, :], AE[:, 4 * q:4 * q + 4, :],
                                            pS[q][:, :].rearrange("p (a b) -> p a b", a=4), ALU.mult)
                    i.then_inc(att, 1)
                for lv in range(5):
                    for q in range(2):
                        x = X[:, 4 * q:4 * q + 4, :]
                        ve.wait_ge(rp, 20 * it + (10 * n + 2 * lv + q + 1))
                        link(v.tensor_tensor(x, pG[q][:, :].rearrange("p (a b) -> p a b", a=4), mask4(M_LEV + 2 * (lv + 1) + d), ALU.mult))
                        v.tensor_tensor(x, x, eye.to_broadcast([P, 4, P]), ALU.add).then_inc(x_ready, 1)
                ve.wait_ge(wu_mm, one_)
                v.tensor_copy(U_t, pyf[:, HEADS:, :]).then_inc(u_sb, 1)
                ve.wait_ge(u_sb, one_)
                ve.wait_ge(ex_ready, one_)
                for st in range(2):
                    cc = st if d == 0 else 1 - st
                    r = slice(64 * cc, 64 * cc + 64)
                    ve.wait_ge(ws_mm, 4 * it + (2 * n + st + 1))
                    for q in range(2):
                        i = v.tensor_tensor(U_t[r, 4 * q:4 * q + 4, :], U_t[r, 4 * q:4 * q + 4, :],
                                            pS[q][r, :].rearrange("p (a b) -> p a b", a=4), ALU.subtract)
                    i.then_inc(vn, 1)
                    ve.wait_ge(ds_mm, 4 * it + (2 * n + st + 1))
                    if ph:
                        o = o_acc[:, :, bass.ds(tile * P + 64 * cc, 64)]
                        v.tensor_tensor(o, o, pG[0][:, :].rearrange("p (h t) -> p h t", h=HEADS), ALU.add)
                    for h in range(HEADS):
                        i = v.scalar_tensor_tensor(state[d][:, h, :], state[d][:, h, :], ex[:, 3 + cc, h:h + 1],
                                                   pyf[:, h, :], ALU.mult, ALU.add)
                    i.then_inc(s_upd, 1)

            PER_BODY = 2 + 10
            for ph in range(2):
                if ph:
                    link(v.memset(o_acc, 0.0))
                with ve.Fori(0, 2) as it:
                    ch.loop(it, 2 * PER_BODY)
                    for d in range(2):
                        scan_body(ph, it, d)
                    ch.end(2)
            ve.wait_ge(o_std, 1)
            link(v.reciprocal(hn, hn))
            link(v.tensor_tensor(o_acc, o_acc, hn, ALU.mult))
            link(v.tensor_scalar(o_acc, o_acc, out_g[:, 0:1], None, ALU.mult))
            v.tensor_tensor(o_acc, o_acc, zs, ALU.mult).then_inc(o_norm, 1)
            h_low(4, o_acc)
            with ve.Fori(0, NC // RING) as n:
                for j in range(RING):
                    split_lo(n, KD + NKV + NIN, j + AHEAD)
                    ve.wait_ge(block_done, RING * n + (KD + NKV + NIN + j + 1 + RING))
                    x = res[0][:, bass.ds(RING * n + j, 1), :].rearrange("p o t -> p (o t)")
                    v.scalar_tensor_tensor(x, pS[j % 2][:, 0:T], gate1[:, bass.ds(RING * n + j, 1)],
                                           x, ALU.mult, ALU.add).then_inc(evacuated, 1)
            ve.wait_ge(evacuated, E3 + 2)
            v.memset(mark[:, 6:7], 0.0).then_inc(y_res, NC)
            norm(6, res[0], 1, 1, 0)
            h_low(5, nrm)
            peer(2, K2, E3, True)
            ve.wait_ge(block_done, RING + K2 + L0)
            ve.wait_ge(res_in, 48)
            add_branch(4, res[0], y_chunk, 1, 5, 0, fin_ready)
            ve.wait_ge(std_ready, 8)
            link(v.reciprocal(inv_std, std))
            link(v.tensor_tensor(hn, res[0], inv_std.unsqueeze(1).to_broadcast([P, NC, T]), ALU.mult))
            v.tensor_tensor(nrm, hn, fin_g2[:, :].unsqueeze(2).to_broadcast([P, NC, T]), ALU.mult).then_inc(normed, 1)

        @block.gpsimd
        def _(pool):
            g_ = nc.gpsimd
            g_.iota(iota[:, :], pattern=[[1, P]], base=0, channel_multiplier=0,
                    allow_small_or_imprecise_dtypes=True).then_inc(ready, 1)
            pool.wait_ge(normed, 2)
            pool.dma_start(a["x_res"], res[0]).then_inc(spilled, 16)
            pool.dma_start(a["x_h"], nrm).then_inc(spilled, 16)
            pool.wait_ge(normed, 4)
            pool.dma_start(a["c_res"], res[1]).then_inc(spilled, 16)

            def peer(g):
                pool.wait_ge(h_split, (1, 2, 6)[g])
                pool.dma_start(keys, a["keysT"][g // 2]).then_inc(keys_in, 16)
                if g == 0:
                    pool.wait_ge(ready, 3)
                with pool.Fori(0, T // 8) as n:
                    for j in range(2):
                        pool.wait_ge(gates_sb, 2 * n + (64 * g + j + 3))
                        x = buf[:, :, bass.ds(8 * n + 4 * j, 4)]
                        g_.tensor_tensor(x, x, g4[j][:, :, :], ALU.mult).then_inc(gated, 1)
            g_.memset(pmark[:, :], 0.0).then_inc(gated, 2)
            pool.wait_ge(spilled, 48)
            peer(0)
            pool.wait_ge(block_done, RING + L0)
            pool.dma_start(hn, a["x_h"]).then_inc(h_in, 16)
            pool.dma_start(res[1], a["c_res"]).then_inc(res_in, 16)
            pool.wait_ge(fin_ready, 1)
            pool.dma_start(a["c_res"], res[1]).then_inc(spilled, 16)
            pool.wait_ge(spilled, 64)
            peer(1)
            pool.wait_ge(block_done, RING + KD)
            pool.dma_start(res[0], a["x_res"]).then_inc(res_in, 16)
            pool.dma_start(res[1], a["c_res"]).then_inc(c_in, 16)
            for dst, src in ((masks, a["masks"]), (cw, a["conv_wT"]), (w_ab, a["w_abT"]), (ab_c[:, 0:2], a["ab_rows"]),
                             (ab_c[:, 2], a["a_log"]), (out_g, a["out_gT"]), (fin_g2[:, :], a["final_gT"])):
                pool.dma_start(dst, src).then_inc(consts2_in, 16)

            def scan_body(ph, it, d):
                n = 2 * it + (4 * ph + d + 1)
                pool.wait_ge(kv_sb, n)
                pool.wait_ge(ex_ready, n)
                bc = lambda i: ex[:, i].unsqueeze(2).to_broadcast([P, HEADS, P])
                g_.tensor_tensor(KG, K_t, bc(1), ALU.mult)
                g_.tensor_tensor(K_t, K_t, bc(0), ALU.mult)
                g_.tensor_tensor(V_t, V_t, bc(2), ALU.mult).then_inc(kvb, 1)
            for ph in range(2):
                with pool.Fori(0, 2) as it:
                    for d in range(2):
                        scan_body(ph, it, d)
            pool.wait_ge(normed, 7)
            pool.dma_start(a["x_res"], res[0]).then_inc(spilled, 16)
            pool.wait_ge(spilled, 80)
            peer(2)
            pool.wait_ge(block_done, RING + K2 + L0)
            pool.dma_start(res[0], a["x_res"]).then_inc(res_in, 16)
            pool.wait_ge(normed, 8)
            pool.dma_start(out, nrm).then_inc(out_done, 16)
            pool.wait_ge(out_done, 16)

        @block.tensor
        def _(pe):
            t_ = nc.tensor
            pe.wait_ge(ready, 3)
            pe.wait_ge(silu_done, 1)
            cs = small[:, 160:160 + 2 * NC].rearrange("p (c b) -> p c b", b=2)
            t_.matmul(pS[0][:, 0:2], ones_mean, inv_d[:, :].to_broadcast([P, 2]), start=True, stop=True).then_inc(mod_done, RING)

            def adaln(L, g0, groups):
                with pe.Fori(0, groups // 2) as n:
                    for i in range(2):
                        m = 2 * n + (L * N_GRP + g0 + i)
                        for j in range(RING):
                            pe.wait_ge(mod_in[j], m * 16 + 16)
                            for c in range(2):
                                mm = t_.matmul(pS[i][0:2, :], cs[:, 2 * j + c, :], mod_slot(j)[:, c, :],
                                               start=(j == 0 and c == 0), stop=(j == RING - 1 and c == 1))
                            mm.then_inc(mod_done, 1)
                        pe.wait_ge(row_ready, m + 1)
                        for q in range(GRP // P):
                            mm = t_.matmul(pG[L][:, bass.ds(16 * n + (8 * (g0 + i) + 2 * q), 2)], row[i][:, q * P:(q + 1) * P], ident[0:2, 0:2],
                                           start=True, stop=True, skip_group_check=True)
                        mm.then_inc(mods_T, 1)

            adaln(0, 0, N_GRP)
            t_.matmul(pS[0][:, 0:2], ones_mean, inv_d[:, :].to_broadcast([P, 2]), start=True, stop=True).then_inc(block_done, RING)
            t_.matmul(pS[0][:, 0:2], ones_mean, inv_d[:, :].to_broadcast([P, 2]), start=True, stop=True).then_inc(evacuated, 2)
            t_.matmul(pS[0][:, 0:2], ones_mean, inv_d[:, :].to_broadcast([P, 2]), start=True, stop=True).then_inc(gates_mm, 4)

            def norm(k):
                pe.wait_ge(squares, k + 1)
                if k == 0:
                    pe.wait_ge(mod_ready, 1)
                for c in range(NC):
                    mm = t_.matmul(pG[0][:, 0:T], ones_mean, sq[:, c, :], start=(c == 0), stop=(c == NC - 1))
                mm.then_inc(mean_sq, 1)

            def pool_project(k):
                pe.wait_ge(pooled_ready, k + 1)
                for g in range(4):
                    for o in range(2):
                        for i in range(2):
                            mm = t_.matmul(pY[:, g, o * T:(o + 1) * T], pool_w[:, 4 * g + 2 * i + o, :], pooled[:, 2 * g + i, :],
                                           start=(i == 0), stop=(i == 1), skip_group_check=True)
                mm.then_inc(pool_mm, 1)

            def s_block(n, k0, e0, j, w=T):
                slot = (k0 + j) % RING
                out = pS[j % 2][:, 0:w]
                pe.wait_ge(lo_ready, RING * n + (k0 + j + 1 + RING))
                pe.wait_ge(evacuated, RING * n + (e0 + j + 1))
                for c in range(NC):
                    t_.matmul(out, hi[slot][:, c, :], h_hi[:, c, :], start=(c == 0), stop=False)
                    t_.matmul(out, hi[slot][:, c, :], h_lo[:, c, :], start=False, stop=False)
                    mm = t_.matmul(out, lo[slot][:, c, :], h_hi[:, c, :], start=False, stop=(c == NC - 1))
                mm.then_inc(block_done, 1)
                return mm

            def s_blocks(k, e, nb):
                with pe.Fori(0, nb // RING) as n:
                    for j in range(RING):
                        s_block(n, k, e, j)

            def peer(g, k0, e0, last):
                pe.wait_ge(h_split, (1, 2, 6)[g])
                s_blocks(k0, e0, NQ)
                pe.wait_ge(evacuated, 2 + e0 + NQ)
                pe.wait_ge(keys_in, 16 * (g + 1))
                if g == 1:
                    pe.wait_ge(fin_ready, 1)
                for r in range(NT):
                    if r:
                        pe.wait_ge(scores_read, NT * g + r)
                    for q in range(NQ):
                        mm = t_.matmul(pY[:, q // 4, (q % 4) * P:(q % 4 + 1) * P], qT[:, q, r * P:(r + 1) * P], keys[:, q, :],
                                       start=True, stop=True, skip_group_check=True)
                    mm.then_inc(scores_done, 1)
                s_blocks(k0 + NQ, e0 + NQ, NE)
                pe.wait_ge(picks_ready, g + 1)
                pe.wait_ge(gated, 2 + 64 * g)
                for q, (dst, off) in enumerate([(pG[0], 0), (pG[0], T), (pG[1], 0)]):
                    for r in range(NT):
                        mm = t_.transpose(dst[:, off + r * P:off + (r + 1) * P], picks[q][:, r * P:(r + 1) * P], ident[:, :])
                mm.then_inc(picksT, 1)
                with pe.Fori(0, N_OCT // 2) as n:
                    for k in range(4):
                        o, q = k // 2, k % 2
                        at_ = 4 * n + (2 * N_OCT * g + k + 1)
                        pe.wait_ge(onehot, at_)
                        pe.wait_ge(rows_gated, at_)
                        pe.wait_ge(gates_sb, at_)
                        for t in range(QUAD):
                            mm = t_.matmul(pG[q][:, t * P:(t + 1) * P], second_rows(o)[:, QUAD * q + t, :].bitcast(F32),
                                           gated1[:, 8 * o + QUAD * q + t, :], start=True, stop=True, skip_group_check=True)
                        mm.then_inc(gates_mm, 1)
                kv = k0 + NQ + NE
                def v_block(n, b0, j, first, lastb):
                    slot = (kv + j) % RING
                    pe.wait_ge(lo_ready, (RING * n + (kv + b0 + j + 1 + RING)) if n is not None else kv + b0 + j + 1 + RING)
                    pe.wait_ge(w_lo, (RING * n + (NE * g + b0 + j + 1)) if n is not None else NE * g + b0 + j + 1)
                    for c in range(NC):
                        o = pY[:, c // 2, (c % 2) * T:(c % 2) * T + T]
                        w1, w2 = h_hi[:, j, :], h_lo[:, j, :]
                        t_.matmul(o, hi[slot][:, c, :], w1, start=first and c % 2 == 0, stop=False, skip_group_check=True)
                        t_.matmul(o, hi[slot][:, c, :], w2, start=False, stop=False, skip_group_check=True)
                        mm = t_.matmul(o, lo[slot][:, c, :], w1, start=False, stop=lastb, skip_group_check=True)
                    mm.then_inc(block_done, 1)
                for j in range(RING):
                    v_block(None, 0, j, j == 0, False)
                with pe.Fori(0, NE // RING - 1) as n:
                    for j in range(RING):
                        v_block(n, RING, j, False, False)

            for k in range(2):
                norm(2 * k)
                adaln(1, k * N_GRP // 2, N_GRP // 2)
                pool_project(k)
                norm(2 * k + 1)
            peer(0, 0, 0, False)
            peer(1, L0, NQ + NE, False)

            def ab_project(k, first):
                pe.wait_ge(normed, 5 + k)
                for r in range(NT):
                    for c in range(NC):
                        mm = t_.matmul(pG[1][:, (2 * k + r) * 32:(2 * k + r + 1) * 32], nrm[:, c, r * P:(r + 1) * P], w_ab[:, c, :],
                                       start=(c == 0), stop=(c == NC - 1), skip_group_check=True)
                mm.then_inc(ab_mm, 1)

            pe.wait_ge(fin_ready, 2)
            pe.wait_ge(consts2_in, 16 * 7)
            norm(4)
            ab_project(0, True)
            pe.wait_ge(h_split, 3)
            s_blocks(KD, E2, NKV)
            norm(5)
            ab_project(1, False)
            pe.wait_ge(h_split, 4)
            s_blocks(KD + NKV, E2 + NKV, NIN)
            for r in range(3):
                pe.wait_ge(l2_sq, r + 1)
                if r:
                    pe.wait_ge(l2_std, r)
                for b in range(4):
                    mm = t_.matmul(pY[:, b, :], ones_mean, sq[:, 2 * b:2 * b + 2, :].rearrange("p a b -> p (a b)"), start=True, stop=True)
                mm.then_inc(l2_mm, 1)

            def scan_body(ph, it, d):
                n = 4 * ph + d
                one_ = 2 * it + (n + 1)
                tile = it if d == 0 else it * -1 + 1
                g_ = gs[:, 16 * d:16 * d + 8]
                lb = gs[:, 16 * d + 8:16 * d + 16]
                pyf = pY[:, :, :].rearrange("p a (b c) -> p (a b) c", c=P)
                psf = [pS[h // 4][:, (h % 4) * P:(h % 4 + 1) * P] for h in range(HEADS)]
                pe.wait_ge(staged, one_)
                for i, m in enumerate((M_CUM + d, M_CHUNK, M_SEG, M_SEG + 1)):
                    mm = t_.matmul(pG[0][:, 8 * i:8 * i + 8], masks[:, m, :], g_, start=True, stop=True, skip_group_check=True)
                mm.then_inc(small_mm, 1)
                for h in range(HEADS):
                    t_.transpose(pyf[:, h, :], kT[:, h, :], ident[:, :])
                    mm = t_.transpose(pyf[:, HEADS + h, :], X[:, h, :], ident[:, :])
                mm.then_inc(trans_mm, 1)
                for h in range(HEADS):
                    mm = t_.matmul(psf[h], kT[:, h, :], kT[:, h, :], start=True, stop=True, skip_group_check=True)
                mm.then_inc(kk_mm, 1)
                pe.wait_ge(kv_sb, one_)
                for h in range(HEADS):
                    t_.matmul(pyf[:, h, :], g_[:, h:h + 1].to_broadcast([P, P]), masks[:, M_CUM + d, :], start=True, stop=False, skip_group_check=True)
                    mm = t_.matmul(pyf[:, h, :], lb[:, h:h + 1].to_broadcast([P, P]), ident[:, :], start=False, stop=True, skip_group_check=True)
                mm.then_inc(rb_mm, 1)
                if ph:
                    for h in range(HEADS):
                        mm = t_.matmul(pyf[:, HEADS + h, :], g_[:, h:h + 1].to_broadcast([P, P]), masks[:, M_CUM + d, :], start=True, stop=True, skip_group_check=True)
                    mm.then_inc(r_mm, 1)
                pe.wait_ge(b_ready, one_)
                for h in range(HEADS):
                    mm = t_.transpose(pyf[:, h, :], BE[:, h, :], ident[:, :])
                mm.then_inc(bt_mm, 1)
                if ph:
                    for h in range(HEADS):
                        mm = t_.matmul(psf[h], kT[:, h, :], conv_x[:, h, bass.ds(tile * P, P)], start=True, stop=True, skip_group_check=True)
                    mm.then_inc(kq_mm, 1)
                pe.wait_ge(e0, one_)
                if ph:
                    pe.wait_ge(er, 2 * it + d + 1)
                for lv in range(5):
                    for q in range(2):
                        if lv:
                            pe.wait_ge(e_sb, 20 * it + (10 * n + 2 * (lv - 1) + q + 1))
                        for h in range(4 * q, 4 * q + 4):
                            mm = t_.matmul(pG[q][:, (h % 4) * P:(h % 4 + 1) * P], BE[:, h, :], ET[:, h, :], start=True, stop=True, skip_group_check=True)
                        mm.then_inc(rp, 1)
                    for q in range(2):
                        pe.wait_ge(x_ready, 20 * it + (10 * n + 2 * lv + q + 1))
                        for h in range(4 * q, 4 * q + 4):
                            mm = t_.matmul(pyf[:, h, :], X[:, h, :], E[:, h, :], start=True, stop=True, skip_group_check=True)
                            if lv < 4:
                                mm = t_.matmul(pyf[:, HEADS + h, :], E[:, h, :], X[:, h, :], start=True, stop=True, skip_group_check=True)
                        mm.then_inc(e_mm, 1)
                pe.wait_ge(e_sb, 20 * it + (10 * n + 10))
                pe.wait_ge(kvb, one_)
                for h in range(HEADS):
                    t_.matmul(pyf[:, h, :], K_t[:, h, :], E[:, h, :], start=True, stop=True, skip_group_check=True)
                    mm = t_.matmul(pyf[:, HEADS + h, :], E[:, h, :], V_t[:, h, :], start=True, stop=True, skip_group_check=True)
                mm.then_inc(wu_mm, 1)
                pe.wait_ge(wt_sb, one_)
                if ph:
                    pe.wait_ge(att, 2 * it + d + 1)
                for st in range(2):
                    cc = st if d == 0 else 1 - st
                    r = slice(64 * cc, 64 * cc + 64)
                    pe.wait_ge(s_upd, 4 * it + (2 * n + st + 1))
                    for h in range(HEADS):
                        mm = t_.matmul(psf[h][r, :], WT[:, h, r], state[d][:, h, :], start=True, stop=True, skip_group_check=True)
                    mm.then_inc(ws_mm, 1)
                    pe.wait_ge(vn, 4 * it + (2 * n + st + 1))
                    for h in range(HEADS):
                        if ph:
                            o = pG[0][:, 64 * h:64 * h + 64]
                            t_.matmul(o, state[d][:, h, :], QG[:, h, r], start=True, stop=False, skip_group_check=True)
                            t_.matmul(o, U_t[r, h, :], AE[r, h, r], start=False, stop=True, skip_group_check=True)
                        mm = t_.matmul(pyf[:, h, :], KG[r, h, :], U_t[r, h, :], start=True, stop=True, skip_group_check=True)
                    mm.then_inc(ds_mm, 1)

            pe.wait_ge(gl_done, 1)
            for ph in range(2):
                with pe.Fori(0, 2) as it:
                    for d in range(2):
                        scan_body(ph, it, d)
            pe.wait_ge(o_sq, 1)
            for b in range(4):
                mm = t_.matmul(pY[:, b, :], ones_mean, sq[:, 2 * b:2 * b + 2, :].rearrange("p a b -> p (a b)"), start=True, stop=True)
            mm.then_inc(o_mm, 1)
            pe.wait_ge(h_split, 5)
            s_blocks(KD + NKV + NIN, E3 - NC, NC)
            norm(6)
            peer(2, K2, E3, True)
            norm(7)


def blocks_of(m):
    return m.reshape(NC, P, -1, P).transpose(2, 1, 0, 3)


def chan(v):
    return np.moveaxis(v.reshape(v.shape[:-1] + (NC, P)), -1, 0)


def chunk_masks():
    r, c = np.arange(P)[:, None], np.arange(P)[None, :]
    same = r // 64 == c // 64
    z = np.zeros((P, P))
    m = [same & (r <= c), same & (r >= c), same, (r < 64) | (z > 0), (r >= 64) | (z > 0)]
    m += [np.where(x, 0.0, -1e30) for x in (same & (r < c), same & (r > c), same & (r <= c), same & (r >= c))]
    for lv in range(6):
        s = 2 ** lv
        x = (r // (2 * s) == c // (2 * s)) & (r % (2 * s) >= s) & (c % (2 * s) < s)
        m += [x, x.T]
    return np.ascontiguousarray(np.stack([np.asarray(x, np.float32) for x in m], 1))


def inverse_counts():
    out = np.zeros((2 * NC, T), np.float32)

    def line(n, w):
        t = np.arange(n)
        return np.clip(t - w // 2 + w, 0, n) - np.clip(t - w // 2, 0, n)
    for g, w in enumerate(WINDOWS):
        out[2 * g:2 * g + 2] = (1.0 / (line(ROWS, w)[:, None] * line(GRID_W, w)[None, :])).reshape(-1)
        out[NC + 2 * g:NC + 2 * g + 2] = 1.0 / line(T, w)
    return np.ascontiguousarray(np.broadcast_to(out, (P, 2 * NC, T)))


def kernel(**x):
    import concourse.bacc as bacc
    from concourse.bass_utils import run_bass_kernel_spmd
    x = {k: np.asarray(v) for k, v in x.items()}
    f = np.ascontiguousarray
    peer = [np.concatenate([blocks_of(x["peer_wq"][L]), blocks_of(x["peer_u"][L].T),
                            x["peer_v"][L].reshape(NE, P, NC, P)]) for L in range(DEPTH)]
    sign = np.broadcast_to(np.array([1, -1], np.float32)[None, :, None], (2, 2, HEADS)).reshape(-1)
    bias = np.stack([x["dn_dt_bias"][0], np.zeros((2, HEADS), np.float32)], 1).reshape(-1)
    alog = np.stack([x["dn_a_log"][0], np.zeros((2, HEADS), np.float32)], 1).reshape(-1)
    arrays = {
        "ident": np.eye(P, dtype=np.float32),
        "cT": f(chan(np.stack([x["c"][0], x["c_ctx"]])).transpose(0, 2, 1).reshape(P, 2 * NC)),
        "mod_bT": f(np.moveaxis(x["mod_b"].reshape(DEPTH * NMOD, P), 1, 0)),
        "gainT": f(chan(np.stack([x["norm1_g"], x["norm2_g"]], 1)).reshape(P, -1)),
        "pool_scaleT": f(chan(x["pool_scale"][0])),
        "xT": f(chan(x["x"][0]).transpose(0, 2, 1)),
        "ctxT": f(chan(x["ctx"][0]).transpose(0, 2, 1)),
        "counts": inverse_counts(),
        "pool_wT": f(x["pool_w"][0].reshape(4, 2, P, 2, P).transpose(2, 0, 1, 3, 4).reshape(P, 16, P)),
        "mod_wT": f(x["mod_w"].reshape(DEPTH, RING, 2, P, N_GRP, GRP).transpose(0, 4, 1, 3, 2, 5).reshape(-1, P, 2, GRP)),
        "keysT": f(x["peer_keys"].reshape(DEPTH, NQ, NKEYS, P).transpose(0, 3, 1, 2)),
        "masks": chunk_masks(),
        "conv_wT": f(x["dn_conv_w"][0].reshape(5, 3 * HEADS, P).transpose(2, 0, 1)),
        "w_abT": f(x["dn_w_in"][0][:, 4 * D:].reshape(NC, P, 4 * HEADS).transpose(1, 0, 2)),
        "ab_rows": f(np.broadcast_to(np.stack([sign, bias]), (P, 2, 4 * HEADS))),
        "a_log": f(np.broadcast_to(alog, (P, 4 * HEADS))),
        "out_gT": f(x["dn_norm_g"][0].reshape(P, 1)),
        "final_gT": f(chan(x["final_g"])),
        "blocks": f(np.concatenate([peer[0], blocks_of(x["dn_w_in"][0][:, :4 * D]), blocks_of(x["dn_w_out"][0]), peer[1]])),
    }
    nc = bacc.Bacc("TRN2", target_bir_lowering=False, num_devices=1)
    aps = {k: nc.dram_tensor("in_" + k, v.shape, mybir.dt.from_np(v.dtype), kind="ExternalInput").ap() for k, v in arrays.items()}
    for k in ("x_res", "x_h", "c_res"):
        aps[k] = nc.dram_tensor("spill_" + k, (P, NC, T), F32, kind="Internal").ap()
    out = nc.dram_tensor("out", (P, NC, T), F32, kind="ExternalOutput").ap()
    build(nc, aps, out)
    r = run_bass_kernel_spmd(nc, [{"in_" + k: v for k, v in arrays.items()}], core_ids=[0]).results[0]
    return np.ascontiguousarray(np.asarray(r["out"]).transpose(2, 1, 0).reshape(1, T, D))
```

```python
from contextlib import ExitStack

import numpy as np
import concourse.bass as bass
import concourse.mybir as mybir

F32 = mybir.dt.float32
F32R = mybir.dt.float32r
BF16 = mybir.dt.bfloat16
U32 = mybir.dt.uint32
ACT = mybir.ActivationFunctionType
ALU = mybir.AluOpType
AX = mybir.AxisListType

P = 128
D = 1024
NC = D // P
T = 256
DEPTH = 2
GRID_W = 64
ROWS = T // GRID_W
EPS = 1e-6
WINDOWS = (2, 4, 8, 16)
HEADS = 8
TOPK = 16
NKEYS = 128
NT = T // P
NQ = 2 * HEADS
NE = NKEYS
NMOD = 6 * NC
MOD_RING = 8
GRP = 512
N_GRP = 6 * D // GRP
NIN = 4 * NC
OCTET, QUAD = 8, 4
N_OCT = T // OCTET
ACT_GATED = 5
RING = 4
AHEAD = 2

L0 = NQ + 2 * NE
W_IN = L0
W_OUT = L0 + NIN
L1 = L0 + NIN + NC
NBLOCKS = L1 + L0

RECTS = [(0, 1), (1, 2), (2, 4), (4, 8), (8, 16)]
RECTS = [(lo, hi, TOPK // (lo + 1)) for lo, hi in RECTS]
PAIRS = [n for lo, hi, n in RECTS for a in range(lo, hi)]
PAIRS[8:] = [1] * 8
OFF = [sum(PAIRS[:a]) for a in range(TOPK)]
NCAND = sum(PAIRS)
TAIL = 8


def build(nc, a, out):
    ctx = ExitStack()
    with ctx:
        def sb(name, shape, dt=F32):
            return ctx.enter_context(nc.sbuf_tensor(name, shape, dt))

        def sem(name):
            return ctx.enter_context(nc.semaphore(name))

        buf = sb("buf", [P, NE, T])
        h_hi = sb("h_hi", [P, NC, T], F32R)
        h_lo = sb("h_lo", [P, NC, T], F32R)
        raw = [sb(f"raw{i}", [P, NC, P]) for i in range(RING)]
        hi = [sb(f"hi{i}", [P, NC, P], F32R) for i in range(RING)]
        lo = [sb(f"lo{i}", [P, NC, P], F32R) for i in range(RING)]
        mods = sb("mods", [P, DEPTH, NMOD, 2])
        ident = sb("ident", [P, P])
        iota = sb("iota", [P, P])
        eps = sb("eps", [P, 1])
        pmark = sb("pmark", [P, 1])
        table = sb("table", [P, 16])
        gated1 = sb("gated1", [P, 16, P])
        one = sb("one", [P, 1])
        eps_q = sb("eps_q", [P, 1])
        fin_g2 = sb("fin_g2", [P, NC])
        mark = sb("mark", [P, 16])
        gT = sb("gT", [P, T])
        g4 = [sb(f"g4_{i}", [P, NKEYS, 4]) for i in range(2)]
        i1T, i2T = (hi[RING - 1][:, 2 * i:2 * i + 2, :].rearrange("p a b -> p (a b)") for i in range(2))
        flat = buf[:, :, :].rearrange("p b t -> p (b t)")

        def region(block, shape, dt=F32):
            n = int(np.prod(shape))
            if dt == BF16:
                n //= 2
            v = flat[:, block * T:block * T + n]
            if dt != F32:
                v = v.bitcast(dt)
            names = "abc"[:len(shape)]
            if len(shape) > 1:
                v = v.rearrange(f"p ({' '.join(names)}) -> p {' '.join(names)}",
                                **{c: s for c, s in zip(names[1:], shape[1:])})
            return v

        def at(off, *shape):
            v = flat[:, off:off + int(np.prod(shape))]
            if len(shape) > 1:
                names = "abc"[:len(shape)]
                v = v.rearrange(f"p ({' '.join(names)}) -> p {' '.join(names)}",
                                **{c: s for c, s in zip(names[1:], shape[1:])})
            return v

        res = [region(0, (NC, T)), region(116, (NC, T))]
        sq = region(84, (NC, T))
        hn = region(92, (NC, T))
        nrm = region(100, (NC, T))
        inv_std = region(108, (T,))
        std = region(109, (T,))
        pooled = region(8, (NC, T))
        counts = region(16, (2 * NC, T))
        pool_w = region(32, (4 * 4, P))
        box = [region(40, (2, 512)), region(44, (2, 512))]
        small = region(48, (1024,))
        row = [region(52 + 2 * i, (GRP,))[0:2] for i in range(2)]
        conv_x = region(8, (3 * HEADS, T))
        zs = region(32, (HEADS, T))
        conv_c = region(40, (2 * HEADS, T))
        state = [at(14336 + 1024 * i, HEADS, P) for i in range(2)]
        masks = at(16384, 21, P)
        pads = [at(19456 + 264 * i, T + 4) for i in range(4)]
        cw = at(20512, 5, 3 * HEADS)
        w_ab = at(20640, NC, 4 * HEADS)
        ab_c = at(20896, 3, 4 * HEADS)
        glog = at(20992, 4, 4 * HEADS)
        gtmp = at(21120, 4, 4 * HEADS)
        neg_c = at(21280, HEADS)
        ex = [at(o, 5, HEADS) for o in (21288, 21376)]
        out_g = at(21360, 1)
        work = [at(21504 + 1024 * i, HEADS, P) for i in range(10)]
        WT1, X, BE, E, ET, K_t, KG0, V_t, WT0, U0 = work
        o_acc = region(40, (HEADS, T))
        WT = [WT0, WT1]
        U_t = [U0, at(19456, HEADS, P)]
        KG = [KG0, gated1[:, 0:HEADS, :]]
        QG = [at(13312, HEADS, P), gated1[:, HEADS:, :]]
        AE = [[at(12288 + 512 * q, 4, P) for q in range(2)],
              [g4[q][:, :, :].rearrange("p b t -> p (b t)").rearrange("p (a b) -> p a b", a=4) for q in range(2)]]
        BODIES = [(i // 4, (i // 2) % 2 if i % 2 == 0 else 1 - (i // 2) % 2, i % 2) for i in range(8)]
        M_CUM, M_CHUNK, M_SEG, M_STRICT, M_INCL, M_LEV = 0, 2, 3, 5, 7, 9

        keys = region(80, (NQ, NKEYS))
        rt = region(88, (1024,))
        top_idx = region(93, (16, 3 * TOPK))
        top = [region(92, (16, TOPK))] + [top_idx[:, :, q * TOPK:(q + 1) * TOPK] for q in (2, 0, 1)]
        qT = region(96, (NQ, T))
        sc = region(112, (2 * HEADS, 2, NKEYS))

        pY = ctx.enter_context(nc.psum_tensor("pY", [P, 4, 512], F32))
        pS = [ctx.enter_context(nc.psum_tensor(f"pS{i}", [P, 512], F32)) for i in range(2)]
        pG = [ctx.enter_context(nc.psum_tensor(f"pG{i}", [P, 512], F32)) for i in range(2)]
        inv_d = sb("inv_d", [P, 1])
        ones_mean = inv_d[:, :].to_broadcast([P, P])

        raw_in = [sem(f"raw_in{i}") for i in range(RING)]
        hi_ready = sem("hi_ready")
        lo_ready = sem("lo_ready")
        block_done = sem("block_done")
        evacuated = sem("evacuated")
        consts_in = sem("consts_in")
        tokens_in = sem("tokens_in")
        ready = sem("ready")
        silu_done = sem("silu_done")
        mod_in = [sem(f"mod_in{i}") for i in range(MOD_RING)]
        mod_done = sem("mod_done")
        row_ready = sem("row_ready")
        mods_T = sem("mods_T")
        mod_ready = sem("mod_ready")
        dve = sem("dve")
        squares = sem("squares")
        mean_sq = sem("mean_sq")
        std_ready = sem("std_ready")
        normed = sem("normed")
        pooled_ready = sem("pooled_ready")
        pool_mm = sem("pool_mm")
        res_ready = sem("res_ready")
        h_split = sem("h_split")
        h_hi_ready = sem("h_hi_ready")
        spilled = sem("spilled")
        keys_in = sem("keys_in")
        scores_done = sem("scores_done")
        scores_read = sem("scores_read")
        exp_in = sem("exp_in")
        exp_done = sem("exp_done")
        picks_ready = sem("picks_ready")
        picksT = sem("picksT")
        e_masked = sem("e_masked")
        e_first = sem("e_first")
        first_ready = sem("first_ready")
        rows_gated = sem("rows_gated")
        onehot = sem("onehot")
        gates_mm = sem("gates_mm")
        gates_sb = sem("gates_sb")
        gated = sem("gated")
        w_hi = sem("w_hi")
        w_lo = sem("w_lo")
        res_in = sem("res_in")
        h_in = sem("h_in")
        out_done = sem("out_done")
        fin_ready = sem("fin_ready")

        def first_rows(o):
            return h_lo[:, 4 * (o % 2):4 * (o % 2) + 4, :].rearrange("p c (t k) -> p (c t) k", k=P)

        def second_rows(o):
            return h_hi[:, 4 * (o % 2):4 * (o % 2) + 4, :].rearrange("p c (t k) -> p (c t) k", k=P)

        def mod_slot(j):
            if j < RING:
                return raw[j][:, :, :].rearrange("p c e -> p (c e)").rearrange("p (c e) -> p c e", c=2)
            return region(44 + 4 * j, (2, GRP))

        picks = [g4[i // 2][:, :, :].rearrange("p b t -> p (b t)")[:, (i % 2) * T:(i % 2 + 1) * T] for i in range(3)]
        U_ROUTE = RING * 2 * HEADS
        NEG = -3.0e38

        consts2_in = sem("consts2_in")
        c_in = sem("c_in")
        ab_mm = sem("ab_mm")
        conv_done = sem("conv_done")
        silu_c = sem("silu_c")
        l2_sq = sem("l2_sq")
        l2_mm = sem("l2_mm")
        l2_std = sem("l2_std")
        l2_done = sem("l2_done")
        gl_x = sem("gl_x")
        gl_e = sem("gl_e")
        gl_done = sem("gl_done")
        small_mm = sem("small_mm")
        trans_mm = sem("trans_mm")
        kk_mm = sem("kk_mm")
        expin = sem("expin")
        ex_ready = sem("ex_ready")
        kv_sb = sem("kv_sb")
        kvb = sem("kvb")
        rb_mm = sem("rb_mm")
        r_mm = sem("r_mm")
        be1 = sem("be1")
        be2 = sem("be2")
        ae1 = sem("ae1")
        ae2 = sem("ae2")
        er = sem("er")
        b_ready = sem("b_ready")
        kq_mm = sem("kq_mm")
        att = sem("att")
        bt_mm = sem("bt_mm")
        e0 = sem("e0")
        rp = sem("rp")
        x_ready = sem("x_ready")
        e_mm = sem("e_mm")
        e_sb = sem("e_sb")
        wu_mm = sem("wu_mm")
        wt_sb = sem("wt_sb")
        u_sb = sem("u_sb")
        ws_mm = sem("ws_mm")
        vn = sem("vn")
        ds_mm = sem("ds_mm")
        s_upd = sem("s_upd")
        o_sq = sem("o_sq")
        o_mm = sem("o_mm")
        o_std = sem("o_std")
        o_norm = sem("o_norm")
        y_res = sem("y_res")

        block = ctx.enter_context(nc.Block())

        KD = 2 * L0
        NKV = 2 * HEADS
        K2 = KD + NKV + NIN + NC
        E2 = 2 * (NQ + NE)
        E3 = E2 + NKV + NIN + NC

        class Chain:
            def __init__(self, eng, s):
                self.eng, self.s, self.n, self.base = eng, s, 0, None

            def loop(self, i, per):
                self.base, self.i, self.per, self.start = self.n, i, per, self.n

            def end(self, trips):
                assert self.n - self.base == self.per, (self.n - self.base, self.per)
                self.n, self.base = self.base + self.per * trips, None

            def link(self, ins):
                self.mark(ins)
                self.wait()

            def mark(self, ins):
                self.n += 1
                ins.then_inc(self.s, 1)

            def wait(self):
                self.eng.wait_ge(self.s, self.n if self.base is None else self.i * self.per + self.n)

        @block.sync
        def _(sp):
            for dst, src in ((small[:, 0:2 * NC], a["cT"]), (ident[:, :], a["ident"]),
                             (small[:, 16:16 + DEPTH * NMOD], a["mod_bT"]),
                             (small[:, 112:112 + 2 * DEPTH * NC], a["gainT"]),
                             (small[:, 144:144 + NC], a["pool_scaleT"])):
                sp.dma_start(dst, src).then_inc(consts_in, 16)

            def adaln_weights(n0, n1):
                with sp.Fori(0, n1 - n0) as n:
                    for j in range(MOD_RING):
                        sp.wait_ge(mod_done, MOD_RING * n + (MOD_RING * n0 + j + 1))
                        sp.dma_start(mod_slot(j), a["mod_wT"][bass.ds(MOD_RING * n + (MOD_RING * n0 + j), 1)]
                                     .rearrange("o p c e -> p (o c) e")).then_inc(mod_in[j], 16)

            adaln_weights(0, 3)
            for dst, src in ((res[0], a["xT"]), (res[1], a["ctxT"]), (counts, a["counts"]), (pool_w, a["pool_wT"])):
                sp.dma_start(dst, src).then_inc(tokens_in, 16)
            adaln_weights(3, DEPTH * N_GRP * RING // MOD_RING)

            def stream(k0, d0, n_blocks):
                with sp.Fori(0, n_blocks // RING) as n:
                    for j in range(RING):
                        sp.wait_ge(lo_ready, RING * n + (k0 + j + 1))
                        sp.dma_start(raw[j][:, :, :], a["blocks"][bass.ds(RING * n + (d0 + j), 1)]
                                     .rearrange("o p c e -> p (o c) e")).then_inc(raw_in[j], 16)

            sp.wait_ge(mod_done, MOD_RING + DEPTH * RING * N_GRP)
            stream(0, 0, L0)
            stream(L0, 0, L0)
            stream(KD, W_IN + HEADS, NKV)
            stream(KD + NKV, W_IN, NIN)
            stream(KD + NKV + NIN, W_OUT, NC)
            stream(K2, L1, L0)

        @block.scalar
        def _(act):
            s = nc.scalar
            tables = [0]

            def preload(func):
                s.activation(table[:, tables[0]:tables[0] + 1], eps[:, :], func)
                tables[0] += 1

            act.wait_ge(ready, 3)
            act.wait_ge(consts_in, 16 * 5)
            s.activation(small[:, 160:160 + 2 * NC], small[:, 0:2 * NC], ACT.Silu).then_inc(silu_done, 1)

            def norm(k, x, wait):
                wait()
                s.activation(sq, x, ACT.Square).then_inc(squares, 1)
                act.wait_ge(mean_sq, k + 1)
                if k:
                    act.wait_ge(normed, k)
                s.activation(std, pG[0][:, 0:T], ACT.Sqrt, bias=eps[:, :]).then_inc(std_ready, 1)

            def split_hi(n, k0, j):
                k = RING * n + (k0 + j) if n is not None else k0 + j
                slot = (k0 + j) % RING
                rounds = (k0 + j) // RING + 1
                act.wait_ge(raw_in[slot], (n + rounds) * 16 if n is not None else 16 * rounds)
                act.wait_ge(block_done, k + 1)
                s.copy(hi[slot][:, :, :], raw[slot][:, :, :]).then_inc(hi_ready, 1)

            def h_high(n_normed):
                act.wait_ge(normed, n_normed)
                s.copy(h_hi[:, :, :], nrm).then_inc(h_hi_ready, 1)

            def peer(g, k0, e0, last):
                preload(ACT.Gelu)
                with act.Fori(0, NQ // RING) as n:
                    for j in range(RING):
                        split_hi(n, k0, j + AHEAD)
                        act.wait_ge(block_done, RING * n + (k0 + j + 1 + RING))
                        s.copy(qT[:, bass.ds(RING * n + j, 1), :], pS[j % 2][:, 0:T].unsqueeze(1)).then_inc(evacuated, 1)
                def u_blocks(b0, nb):
                    with act.Fori(0, nb // RING) as n:
                        for j in range(RING):
                            split_hi(n, k0 + NQ + b0, j + AHEAD)
                            act.wait_ge(block_done, RING * n + (k0 + NQ + b0 + j + 1 + RING))
                            s.activation(buf[:, bass.ds(RING * n + (b0 + j), 1), :], pS[j % 2][:, 0:T].unsqueeze(1), ACT.Gelu).then_inc(evacuated, 1)
                act.wait_ge(spilled, (48, 64, 80)[g])
                u_blocks(0, U_ROUTE)
                act.wait_ge(exp_in, g + 1)
                s.activation(top[0], top[0], ACT.Exp).then_inc(exp_done, 1)
                preload(ACT.Gelu)
                u_blocks(U_ROUTE, NE - U_ROUTE)
                def gate_rows(n, o):
                    act.wait_ge(first_ready, 2 * n + (N_OCT * g + o + 1) if n is not None else N_OCT * g + o + 1)
                    for t in range(ACT_GATED):
                        tok = 16 * n + (8 * o + t) if n is not None else 8 * o + t
                        i = s.activation(gated1[:, 8 * (o % 2) + t, :], first_rows(o)[:, t, :].bitcast(F32), ACT.Copy, scale=gT[:, bass.ds(tok, 1)])
                        if t in (QUAD - 1, ACT_GATED - 1):
                            i.then_inc(rows_gated, 1)

                def gates_out(n, o):
                    for q in range(2):
                        k = 2 * o + q
                        act.wait_ge(gates_mm, 4 * n + (2 * N_OCT * g + k + 5) if n is not None else 2 * N_OCT * g + k + 5)
                        act.wait_ge(gated, 4 * n + (2 * N_OCT * g + k + 1) if n is not None else 2 * N_OCT * g + k + 1)
                        s.copy(g4[q][:, :, :], pG[q][:, :].rearrange("p (t b) -> p b t", t=QUAD)).then_inc(gates_sb, 1)

                gate_rows(None, 0)
                with act.Fori(0, N_OCT // 2 - 1) as n:
                    for o in range(2):
                        gate_rows(n, o + 1)
                        gates_out(n, o)
                gate_rows(None, N_OCT - 1)
                gates_out(None, N_OCT - 2)
                gates_out(None, N_OCT - 1)
                kv = k0 + NQ + NE
                act.wait_ge(gated, 2 + 64 * (g + 1))
                def v_body(n, b0, peel):
                    for j in range(RING):
                        b = RING * n + (b0 + j) if n is not None else b0 + j
                        act.wait_ge(block_done, b + (kv + 1))
                        s.copy(w_h(j), buf[:, bass.ds(b, 1), :] if n is not None else buf[:, b:b + 1, :]).then_inc(w_hi, 1)
                        if not (peel and j + AHEAD >= RING):
                            split_hi(n, kv + b0, j + AHEAD)
                nl = NE // RING - (1 if last else 0)
                with act.Fori(0, nl) as n:
                    v_body(n, 0, False)
                if last:
                    v_body(None, NE - RING, True)

            def w_h(j):
                return h_hi[:, j:j + 1, :]

            def init():
                for j in range(AHEAD):
                    split_hi(None, 0, j)

            def adaln(L, g0, groups):
                with act.Fori(0, groups // 2) as n:
                    for i in range(2):
                        m = 2 * n + (L * N_GRP + g0 + i)
                        act.wait_ge(mod_done, m * RING + RING + MOD_RING)
                        s.copy(row[i], pS[i][0:2, :]).then_inc(row_ready, 1)

            adaln(0, 0, N_GRP)
            act.wait_ge(tokens_in, 16 * 4)
            for k in range(2):
                norm(2 * k, res[k], lambda: act.wait_ge(mod_ready, 1))
                adaln(1, k * N_GRP // 2, N_GRP // 2)
                norm(2 * k + 1, res[k], lambda: act.wait_ge(res_ready, k + 1))
            h_high(4)
            init()
            peer(0, 0, 0, False)
            act.wait_ge(h_in, 16)
            s.copy(h_hi[:, :, :], hn).then_inc(h_hi_ready, 1)
            peer(1, L0, NQ + NE, False)

            def s_evac(k0, e0, nb, f):
                with act.Fori(0, nb // RING) as n:
                    for j in range(RING):
                        split_hi(n, k0, j + AHEAD)
                        act.wait_ge(block_done, RING * n + (k0 + j + 1 + RING))
                        f(n, j)

            def to_pads(c0):
                def f(n, j):
                    act.wait_ge(conv_done, RING * n + (c0 + j + 1))
                    s.copy(pads[j][:, 2:2 + T], pS[j % 2][:, 0:T]).then_inc(evacuated, 1)
                return f

            def to_z(n, j):
                s.activation(zs[:, bass.ds(RING * n + j, 1), :], pS[j % 2][:, 0:T].unsqueeze(1), ACT.Silu).then_inc(evacuated, 1)

            norm(4, res[1], lambda: act.wait_ge(c_in, 16))
            h_high(5)
            s_evac(KD, E2, NKV, to_pads(0))
            act.wait_ge(conv_done, RING + NKV)
            s.activation(conv_c, conv_c, ACT.Silu).then_inc(silu_c, 1)
            norm(5, res[0], lambda: act.wait_ge(fin_ready, 2))
            h_high(6)
            s_evac(KD + NKV, E2 + NKV, 3 * HEADS, to_pads(NKV))
            act.wait_ge(conv_done, RING + NKV + 3 * HEADS)
            s.activation(conv_x, conv_x, ACT.Silu).then_inc(silu_c, 1)
            s_evac(KD + NKV + 3 * HEADS, E2 + NKV + 3 * HEADS, HEADS, to_z)
            act.wait_ge(silu_c, 2)
            for r, x in enumerate((conv_c[:, 0:HEADS], conv_x[:, 0:HEADS], conv_x[:, HEADS:2 * HEADS])):
                if r:
                    act.wait_ge(l2_mm, r)
                s.activation(sq, x, ACT.Square).then_inc(l2_sq, 1)
                act.wait_ge(l2_mm, r + 1)
                if r == 2:
                    act.wait_ge(l2_done, 1)
                q_scale = float(P) if r == 1 else 1.0
                s.activation((hn, nrm)[r % 2].rearrange("p c t -> p (c t)"), pY[:, :, :].rearrange("p a b -> p (a b)"), ACT.Sqrt,
                             bias=(eps_q if r == 1 else eps)[:, :], scale=D * q_scale).then_inc(l2_std, 1)
            act.wait_ge(consts2_in, 16 * 7)
            act.wait_ge(gl_x, 1)
            s.activation(ab_c[:, 2], ab_c[:, 2], ACT.Exp).then_inc(gl_e, 1)
            s.activation(gtmp, gtmp, ACT.Exp).then_inc(gl_e, 1)
            act.wait_ge(gl_e, 2)
            s.activation(gtmp, gtmp, ACT.Ln, bias=one[:, :]).then_inc(gl_e, 1)

            def prepare(i, ph, tile, d):
                act.wait_ge(expin, i + 1)
                s.activation(ex[d], ex[d], ACT.Exp).then_inc(ex_ready, 1)
                act.wait_ge(trans_mm, i + 1)
                pyf = pY[:, :, :].rearrange("p a (b c) -> p (a b) c", c=P)
                s.copy(K_t, pyf[:, 0:HEADS, :])
                s.copy(V_t, pyf[:, HEADS:, :]).then_inc(kv_sb, 1)
                act.wait_ge(be1, i + 1)
                for h in range(HEADS):
                    last = s.activation(BE[:, h, :], BE[:, h, :], ACT.Exp, bias=neg_c[:, h:h + 1])
                last.then_inc(be2, 1)
                if ph:
                    act.wait_ge(ae1, i - 3)
                    s.activation(QG[d], pyf[:, HEADS:, :], ACT.Exp).then_inc(er, 1)
                    for h in range(HEADS):
                        a_ = AE[d][h // 4][:, h % 4, :]
                        last = s.activation(a_, a_, ACT.Exp, bias=neg_c[:, h:h + 1])
                    last.then_inc(ae2, 1)
                for lv in range(5):
                    for q in range(2):
                        act.wait_ge(e_mm, 10 * i + 2 * lv + q + 1)
                        last = s.copy(E[:, 4 * q:4 * q + 4, :], pyf[:, 4 * q:4 * q + 4, :])
                        if lv < 4:
                            last = s.copy(ET[:, 4 * q:4 * q + 4, :], pyf[:, 8 + 4 * q:12 + 4 * q, :])
                        last.then_inc(e_sb, 1)
                act.wait_ge(wu_mm, i + 1)
                s.copy(WT[d], pyf[:, 0:HEADS, :]).then_inc(wt_sb, 1)

            act.wait_ge(gl_done, 1)
            act.wait_ge(l2_done, 3)
            preload(ACT.Exp)
            for i, body in enumerate(BODIES):
                prepare(i, *body)
            act.wait_ge(s_upd, 1 + 4 * len(BODIES))
            s.activation(sq, o_acc, ACT.Square).then_inc(o_sq, 1)
            act.wait_ge(o_mm, 1)
            s.activation(hn.rearrange("p c t -> p (c t)"), pY[:, :, :].rearrange("p a b -> p (a b)"), ACT.Sqrt,
                         bias=eps[:, :], scale=float(NC)).then_inc(o_std, 1)
            act.wait_ge(o_norm, 1)
            s.copy(h_hi[:, :, :], o_acc).then_inc(h_hi_ready, 1)
            with act.Fori(0, NC // RING) as n:
                for j in range(RING):
                    split_hi(n, KD + NKV + NIN, j + AHEAD)
            norm(6, res[0], lambda: act.wait_ge(y_res, NC))
            h_high(7)
            peer(2, K2, E3, True)
            act.wait_ge(fin_ready, 3)
            norm(7, res[0], lambda: None)

        @block.vector
        def _(ve):
            v = nc.vector
            ch = Chain(ve, dve)
            link = ch.link
            v.memset(eps[:, :], EPS).then_inc(ready, 1)
            v.memset(inv_d[:, :], 1.0 / D).then_inc(ready, 1)
            v.memset(mark[:, 12:13], 0.0).then_inc(gates_sb, 2)
            v.memset(mark[:, 13:14], 0.0).then_inc(lo_ready, RING)

            ve.wait_ge(consts_in, 16 * 5)
            def adaln(L):
                ve.wait_ge(mods_T, 4 * N_GRP * (L + 1))
                m = mods[:, L]
                bias = small[:, 16 + L * NMOD:16 + (L + 1) * NMOD]
                link(v.tensor_tensor(m, pG[L][:, 0:2 * NMOD].rearrange("p (a b) -> p a b", b=2),
                                     bias.unsqueeze(2).to_broadcast([P, NMOD, 2]), ALU.add))
                for sub in range(2):
                    g = small[:, 112 + (2 * L + sub) * NC:112 + (2 * L + sub + 1) * NC]
                    scale = m[:, (3 * sub + 1) * NC:(3 * sub + 2) * NC]
                    link(v.tensor_scalar(scale, scale, 1.0, None, ALU.add))
                    link(v.tensor_tensor(scale, scale, g.unsqueeze(2).to_broadcast([P, NC, 2]), ALU.mult))
                if L == 0:
                    gate = m[:, 2 * NC:3 * NC]
                    link(v.tensor_tensor(gate, gate, small[:, 144:144 + NC].unsqueeze(2).to_broadcast([P, NC, 2]), ALU.mult))
                v.memset(mark[:, 2 + 8 * L:3 + 8 * L], 0.0).then_inc(mod_ready, 1)

            adaln(0)

            def norm(k, x, layer, sub, which):
                ve.wait_ge(std_ready, k + 1)
                link(v.reciprocal(inv_std, std))
                link(v.tensor_tensor(hn, x, inv_std.unsqueeze(1).to_broadcast([P, NC, T]), ALU.mult))
                for c in range(NC):
                    ins = v.tensor_scalar(nrm[:, c, :], hn[:, c, :], mods[:, layer, (3 * sub + 1) * NC + c, which:which + 1],
                                          mods[:, layer, 3 * sub * NC + c, which:which + 1], ALU.mult, ALU.add)
                ins.then_inc(normed, 1)

            def box_add(dst, x, y):
                link(v.tensor_tensor(dst, x, y, ALU.add))

            def pool_grid():
                for g, w in enumerate(WINDOWS):
                    x = nrm[:, 2 * g:2 * g + 2, :]
                    xr = x.rearrange("p c (r w) -> p c r w", r=ROWS)
                    A, B = (t_[:, :, :].rearrange("p c n -> p (c n)")[:, 0:2 * ROWS * 96]
                            .rearrange("p (c r w) -> p c r w", c=2, r=ROWS) for t_ in box_big)
                    link(v.memset(box_big[0][:, :, :], 0.0))
                    link(v.memset(box_big[1][:, :, :], 0.0))
                    mid = slice(16, 16 + GRID_W)
                    if w == 2:
                        v.tensor_copy(A[:, :, 0:1, mid], xr[:, :, 0:1, :])
                        for cc in range(2):
                            i = v.tensor_tensor(A[:, cc, 1:ROWS, mid], xr[:, cc, 1:ROWS, :], xr[:, cc, 0:ROWS - 1, :], ALU.add)
                        link(i)
                    elif w == 4:
                        for cc in range(2):
                            i = v.tensor_tensor(B[:, cc, 0:ROWS - 1, mid], xr[:, cc, 0:ROWS - 1, :], xr[:, cc, 1:ROWS, :], ALU.add)
                        link(i)
                        for cc in range(2):
                            v.tensor_copy(A[:, cc, 0:1, mid], B[:, cc, 0:1, mid])
                            v.tensor_tensor(A[:, cc, 1:2, mid], B[:, cc, 1:2, mid], xr[:, cc, 0:1, :], ALU.add)
                            v.tensor_tensor(A[:, cc, 2:3, mid], B[:, cc, 2:3, mid], B[:, cc, 0:1, mid], ALU.add)
                            i = v.tensor_tensor(A[:, cc, 3:4, mid], B[:, cc, 1:2, mid], xr[:, cc, 3:4, :], ALU.add)
                        link(i)
                    else:
                        for cc in range(2):
                            i = v.tensor_tensor(B[:, cc, 0:2, mid], xr[:, cc, 0:2, :], xr[:, cc, 2:4, :], ALU.add)
                        link(i)
                        for cc in range(2):
                            i = v.tensor_tensor(A[:, cc, 0:1, mid], B[:, cc, 0:1, mid], B[:, cc, 1:2, mid], ALU.add)
                        link(i)
                        for cc in range(2):
                            i = v.tensor_copy(A[:, cc, 1:ROWS, mid], A[:, cc, 0:1, mid].to_broadcast([P, ROWS - 1, GRID_W]))
                        link(i)
                    A2, B2 = (t_.rearrange("p c r w -> p (c r) w") for t_ in (A, B))
                    if w != 2:
                        link(v.memset(box_big[1][:, :, :], 0.0))
                    line_windows(A2, B2, w, GRID_W, pooled[:, 2 * g:2 * g + 2, :].rearrange("p c (r w) -> p (c r) w", r=ROWS))
                    finish_pool(0, g, x)

            def line_windows(A, B, w, n, out):
                lo_, hi_ = 16 - w, 16 + n + w - 1
                src, dst = A, B
                step = 1
                first = True
                width = 2
                while width <= w:
                    r = w // 2 - width // 2
                    lo_, hi_ = 16 - r, 16 + n + r
                    if first:
                        x0, x1 = src[:, :, lo_ - 1:hi_ - 1], src[:, :, lo_:hi_]
                        first = False
                    else:
                        q = width // 4
                        x0, x1 = src[:, :, lo_ - q:hi_ - q], src[:, :, lo_ + q:hi_ + q]
                    if width == w:
                        link(v.tensor_tensor(out, x0, x1, ALU.add))
                    else:
                        link(v.tensor_tensor(dst[:, :, lo_:hi_], x0, x1, ALU.add))
                    src, dst = dst, src
                    width *= 2

            def finish_pool(which, g, x):
                o = pooled[:, 2 * g:2 * g + 2, :]
                link(v.tensor_tensor(o, o, counts[:, which * NC + 2 * g:which * NC + 2 * g + 2, :], ALU.mult))
                link(v.tensor_tensor(o, o, x, ALU.subtract))

            def pool_line():
                for g, w in enumerate(WINDOWS):
                    x = nrm[:, 2 * g:2 * g + 2, :]
                    A, B = (t_[:, :, 0:T + 32] for t_ in box_big)
                    link(v.memset(box_big[0][:, :, :], 0.0))
                    link(v.memset(box_big[1][:, :, :], 0.0))
                    link(v.tensor_copy(A[:, :, 16:16 + T], x))
                    line_windows(A, B, w, T, pooled[:, 2 * g:2 * g + 2, :])
                    finish_pool(1, g, x)

            box_big = box

            def add_branch(k, x, ps_of, layer, sec, which, signal):
                for c in range(NC):
                    i = v.scalar_tensor_tensor(x[:, c, :], ps_of(c), mods[:, layer, sec * NC + c, which:which + 1],
                                               x[:, c, :], ALU.mult, ALU.add)
                i.then_inc(signal, 1)

            def y_chunk(c):
                return pY[:, c // 2, (c % 2) * T:(c % 2) * T + T]

            for k in range(2):
                norm(2 * k, res[k], 0, 0, k)
                ve.wait_ge(normed, 2 * k + 1)
                (pool_grid if k == 0 else pool_line)()
                v.memset(mark[:, 3:4], 0.0).then_inc(pooled_ready, 1)
                ve.wait_ge(pool_mm, k + 1)
                add_branch(k, res[k], y_chunk, 0, 2, k, res_ready)
                ve.wait_ge(res_ready, k + 1)
                norm(2 * k + 1, res[k], 0, 1, k)
                if k == 0:
                    ve.wait_ge(spilled, 32)

            def split_lo(n, k0, j):
                k = RING * n + (k0 + j) if n is not None else k0 + j
                slot = (k0 + j) % RING
                ve.wait_ge(hi_ready, k + 1)
                v.tensor_tensor(lo[slot][:, :, :], raw[slot][:, :, :], hi[slot][:, :, :].bitcast(F32), ALU.subtract).then_inc(lo_ready, 1)

            def link_max(ins):
                link(ins)
                v.memset(mark[:, 0:1], 0.0)

            def route_unit(u, n, part):
                both = u[:, 0:256]
                without = u[:, 256:512]
                val = u[:, 512:544]
                cand = u[:, 544:600]
                candb = u[:, 608:664]
                best = u[:, 672:688]
                idx = u[:, 704:752].bitcast(U32)
                half = lambda x, hf: x[:, hf * NKEYS:(hf + 1) * NKEYS]
                a = [[val[:, 16 * hf + 8 * r:16 * hf + 8 * r + 8] for r in range(2)] for hf in range(2)]
                a0, a1 = best[:, 0:8], best[:, 8:16]
                if part == 0:
                    link_max(v.tensor_copy(both, sc.rearrange("p u h k -> p u (h k)")[:, bass.ds(n, 1), :].rearrange("p o k -> p (o k)")))
                    v.max(a[0][0], half(both, 0))
                    link_max(v.max(a[1][0], half(both, 1)))
                elif part == 1:
                    for hf in range(2):
                        v.max_index(idx[:, 16 * hf:16 * hf + 8], a[hf][0], half(both, hf))
                        i = v.match_replace(half(without, hf), a[hf][0], half(both, hf), NEG)
                    link_max(i)
                    v.max(a[0][1], half(without, 0))
                    link_max(v.max(a[1][1], half(without, 1)))
                elif part == 2:
                    for hf in range(2):
                        v.max_index(idx[:, 16 * hf + 8:16 * hf + 16], a[hf][1], half(without, hf))
                    for lo_, hi_, nb in RECTS:
                        o = cand[:, OFF[lo_]:OFF[lo_] + (hi_ - lo_) * nb].rearrange("p (a b) -> p a b", b=nb)
                        i = v.tensor_tensor(o, val[:, lo_:hi_].unsqueeze(2).to_broadcast([P, hi_ - lo_, nb]),
                                            val[:, 16:16 + nb].unsqueeze(1).to_broadcast([P, hi_ - lo_, nb]), ALU.add)
                    link_max(i)
                    link_max(v.max(a0, cand[:, 0:NCAND]))
                else:
                    v.max_index(idx[:, 32:40], a0, cand[:, 0:NCAND])
                    link_max(v.match_replace(candb[:, 0:NCAND], a0, cand[:, 0:NCAND], NEG))
                    link_max(v.max(a1, candb[:, 0:NCAND]))
                    link(v.max_index(idx[:, 40:48], a1, candb[:, 0:NCAND]))
                    v.tensor_copy(top[0][:, bass.ds(n, 1), :], best.unsqueeze(1))
                    link(v.tensor_copy(top_idx[:, bass.ds(n, 1), :], idx.unsqueeze(1)))
            UNIT_LINKS = 2 + 2 + 2 + 4

            def peer(g, k0, e0, last):
                kq, ku = k0, k0 + NQ
                with ve.Fori(0, NQ // RING) as n:
                    for j in range(RING):
                        split_lo(n, kq, j + AHEAD)
                if g == 1:
                    ve.wait_ge(spilled, 64)
                for r in range(NT):
                    ve.wait_ge(scores_done, NT * g + r + 1)
                    i = v.tensor_copy(sc[:, 8 * r:8 * r + 8].rearrange("p u h k -> p (u h k)"),
                                      pY[:, :, :].rearrange("p a b -> p (a b)"))
                    i.then_inc(scores_read, 1)
                ve.wait_ge(scores_read, NT * g + NT)
                with ve.Fori(0, 2 * HEADS) as n:
                    ch.loop(n, UNIT_LINKS)
                    for j in range(RING):
                        split_lo(n, ku, j + AHEAD)
                        route_unit(rt, n, j)
                    ch.end(2 * HEADS)
                b = RING * 2 * HEADS
                steps = post_steps()
                for i, st in enumerate(steps):
                    st(g)
                    split_lo(None, ku + b, i + AHEAD)
                b += len(steps)
                while b % RING:
                    split_lo(None, ku + b, AHEAD)
                    b += 1
                assert b <= 88, b
                with ve.Fori(0, (NE - b) // RING) as n:
                    for j in range(RING):
                        split_lo(n, ku + b, j + AHEAD)
                ve.wait_ge(picksT, g + 1)
                v.tensor_copy(gT[:, :], pG[1][:, 0:T])
                v.tensor_copy(i1T, pG[0][:, 0:T])
                link(v.tensor_copy(i2T, pG[0][:, T:2 * T]))
                v.memset(mark[:, 4:5], 0.0)
                with ve.Fori(0, N_OCT // 2) as n:
                    for o in range(2):
                        ve.wait_ge(gates_mm, 4 * n + (2 * N_OCT * g + 2 * o + 2))
                        def onehot_rows(dst, idx, m):
                            return v.tensor_tensor(dst[:, 0:m, :], iota[:, :].unsqueeze(1).to_broadcast([P, m, P]),
                                                   idx[:, bass.ds(16 * n + 8 * o, m)].bitcast(F32).unsqueeze(2).to_broadcast([P, m, P]), ALU.is_equal)
                        onehot_rows(first_rows(o), i1T, ACT_GATED).then_inc(first_ready, 1)
                        onehot_rows(second_rows(o), i2T, OCTET).then_inc(onehot, 1)
                        for t in range(ACT_GATED, OCTET):
                            tok = 16 * n + (8 * o + t)
                            i = v.tensor_scalar(gated1[:, 8 * o + t, :], iota[:, :], i1T[:, bass.ds(tok, 1)].bitcast(F32), gT[:, bass.ds(tok, 1)], ALU.is_equal, ALU.mult)
                        i.then_inc(onehot, 1)
                kv = k0 + NQ + NE
                def v_body(n, b0, peel):
                    for j in range(RING):
                        b = RING * n + (b0 + j) if n is not None else b0 + j
                        ve.wait_ge(w_hi, b + (NE * g + 1))
                        v.tensor_tensor(h_lo[:, j:j + 1, :], buf[:, bass.ds(b, 1), :] if n is not None else buf[:, b:b + 1, :],
                                        h_hi[:, j:j + 1, :].bitcast(F32), ALU.subtract).then_inc(w_lo, 1)
                        if not (peel and j + AHEAD >= RING):
                            split_lo(n, kv + b0, j + AHEAD)
                nl = NE // RING - (1 if last else 0)
                with ve.Fori(0, nl) as n:
                    v_body(n, 0, False)
                if last:
                    v_body(None, NE - RING, True)

            def post_steps():
                A_ = rt[:, 0:256]
                B_ = rt[:, 256:512]
                A3, B3, step3 = (rt[:, o:o + 256].rearrange("p (u k) -> p u k", k=TOPK) for o in (0, 256, 544))
                g16 = rt[:, 512:528]
                g16r = rt[:, 528:544]
                pos = top[1]
                val = top[0]
                hot = region(96, (HEADS, TOPK, TOPK))
                hotm = region(104, (HEADS, TOPK, TOPK))
                def softmax_in(g):
                    link(v.tensor_copy(g16, val[:, :, 0]))
                    v.tensor_tensor(val, val, g16.unsqueeze(2).to_broadcast([P, 16, TOPK]), ALU.subtract).then_inc(exp_in, 1)
                    link(v.tensor_scalar(A3, pos, -(OFF[TAIL] - 1.0), 0.0, ALU.add, ALU.max))
                    link(v.tensor_tensor(B3, pos, A3, ALU.subtract))
                def off_a(m):
                    def f(g):
                        if m < TAIL:
                            link(v.scalar_tensor_tensor(A3, pos, float(OFF[m]), A3, ALU.is_ge, ALU.add))
                        w = float(PAIRS[m - 1] - (m == TAIL))
                        link(v.tensor_scalar(step3, pos, float(OFF[m]), w, ALU.is_ge, ALU.mult))
                        link(v.tensor_tensor(B3, B3, step3, ALU.subtract))
                    return f
                def gather(which, tile, part):
                    pick = (A_ if which == 0 else B_)[:, tile * P:(tile + 1) * P]
                    lst = top[2 + which][:, tile * HEADS:(tile + 1) * HEADS, :]
                    dst = (gi1 if which == 0 else gi2)[:, tile * P:(tile + 1) * P]
                    io = iota[:, 0:TOPK]
                    def f(g):
                        if part == 0:
                            link(v.tensor_tensor(hot.rearrange("p h k a -> p (h k) a"), pick.unsqueeze(2).to_broadcast([P, P, TOPK]),
                                                 io.unsqueeze(1).to_broadcast([P, P, TOPK]), ALU.is_equal))
                        elif part == 1:
                            link(v.tensor_tensor(hotm, hot, lst.unsqueeze(2).to_broadcast([P, HEADS, TOPK, TOPK]), ALU.mult))
                        else:
                            link(v.tensor_reduce(dst.rearrange("p (h k) -> p h k", h=HEADS), hotm, AX.X, ALU.add))
                    return f
                gi1, gi2 = region(112, (256,)), region(113, (256,))
                def softmax_out(g):
                    ve.wait_ge(exp_done, g + 1)
                    link(v.tensor_reduce(g16, val, AX.X, ALU.add))
                    link(v.reciprocal(g16r, g16))
                    link(v.tensor_tensor(val, val, g16r.unsqueeze(2).to_broadcast([P, 16, TOPK]), ALU.mult))
                def done(g):
                    ve.wait_ge(gated, 2 + 64 * g)
                    v.tensor_copy(picks[0][:, :], gi1)
                    v.tensor_copy(picks[1][:, :], gi2)
                    v.tensor_copy(picks[2][:, :], val.rearrange("p u k -> p (u k)")).then_inc(picks_ready, 1)
                return ([softmax_in] + [off_a(m) for m in range(1, TAIL + 1)] +
                        [gather(which, tile, part) for which in range(2) for tile in range(NT) for part in range(3)] +
                        [softmax_out, done])

            def h_low(k, src):
                ve.wait_ge(h_hi_ready, k + 1)
                v.tensor_tensor(h_lo[:, :, :], src, h_hi[:, :, :].bitcast(F32), ALU.subtract).then_inc(h_split, 1)

            h_low(0, nrm)
            adaln(1)
            for j in range(AHEAD):
                split_lo(None, 0, j)
            peer(0, 0, 0, False)
            h_low(1, hn)
            ve.wait_ge(res_in, 16)
            add_branch(2, res[1], y_chunk, 0, 5, 1, fin_ready)
            peer(1, L0, NQ + NE, False)
            ve.wait_ge(block_done, RING + KD)
            ve.wait_ge(res_in, 32)
            add_branch(3, res[0], y_chunk, 0, 5, 0, fin_ready)

            def conv_section(k0, c0, w0, dst, nb):
                with ve.Fori(0, nb // RING) as n:
                    ch.loop(n, RING * 4)
                    for j in range(RING):
                        ve.wait_ge(evacuated, RING * n + (c0 + E2 + j + 3))
                        o = dst[:, bass.ds(RING * n + j, 1), :].rearrange("p o t -> p (o t)")
                        tap = [cw[:, i, bass.ds(RING * n + (w0 + j), 1)] for i in range(5)]
                        link(v.tensor_scalar(o, pads[j][:, 0:T], tap[0], None, ALU.mult))
                        for i in range(1, 5):
                            ins = v.scalar_tensor_tensor(o, pads[j][:, i:i + T], tap[i], o, ALU.mult, ALU.add)
                            if i < 4:
                                link(ins)
                        ins.then_inc(conv_done, 1)
                    ch.end(nb // RING)

            norm(4, res[1], 1, 0, 1)
            h_low(2, nrm)
            ve.wait_ge(consts2_in, 16 * 7)
            v.memset(one[:, :], 1.0)
            v.memset(eps_q[:, :], EPS * P)
            for i in range(4):
                ins = v.memset(pads[i], 0.0)
            ins.then_inc(conv_done, RING)
            conv_section(KD, 0, HEADS, conv_c, NKV)
            ve.wait_ge(ab_mm, 1)
            norm(5, res[0], 1, 0, 0)
            h_low(3, nrm)
            conv_section(KD + NKV, NKV, 0, conv_x, 3 * HEADS)
            for r, x in enumerate((conv_c[:, 0:HEADS], conv_x[:, 0:HEADS], conv_x[:, HEADS:2 * HEADS])):
                ve.wait_ge(l2_std, r + 1)
                norms = (hn, nrm)[r % 2]
                link(v.reciprocal(norms, norms))
                v.tensor_tensor(x, x, norms, ALU.mult).then_inc(l2_done, 1)
            ve.wait_ge(ab_mm, 2)
            rows = lambda i: ab_c[:, i:i + 1, :].to_broadcast([P, 4, 4 * HEADS])
            link(v.tensor_tensor(glog, pG[1][:, 0:P].rearrange("p (a b) -> p a b", a=4), rows(0), ALU.mult))
            link(v.tensor_tensor(glog, glog, rows(1), ALU.add))
            v.scalar_tensor_tensor(gtmp, glog, -1.0, glog, ALU.mult, ALU.min).then_inc(gl_x, 1)
            ve.wait_ge(gl_x, 1)
            link(v.tensor_scalar(glog, glog, 0.0, None, ALU.max))
            ve.wait_ge(gl_e, 3)
            link(v.tensor_tensor(glog, glog, gtmp, ALU.add))
            link(v.tensor_tensor(glog, glog, rows(2), ALU.mult))
            link(v.tensor_scalar(glog, glog, -1.0, None, ALU.mult))
            v.memset(mark[:, 5:6], 0.0).then_inc(gl_done, 1)
            v.memset(state[0], 0.0)
            v.memset(state[1], 0.0).then_inc(s_upd, 1)

            gate1 = mods[:, 1, 2 * NC:3 * NC, 0]

            def mask(i):
                return masks[:, i:i + 1, :].to_broadcast([P, HEADS, P])

            def mask4(i):
                return masks[:, i:i + 1, :].to_broadcast([P, 4, P])

            eye = ident[:, :].unsqueeze(1)

            def scan_piece(i, stage):
                ph, tile, d = BODIES[i]
                st, q, second = stage // 4, (stage // 2) % 2, stage % 2
                k = 4 * i + stage // 2 + 1
                cc = st if d == 0 else 1 - st
                r = slice(64 * cc, 64 * cc + 64)
                heads = slice(4 * q, 4 * q + 4)
                if not second:
                    ve.wait_ge(ws_mm, k)
                    v.tensor_tensor(U_t[d][r, heads, :], U_t[d][r, heads, :],
                                    pS[0][r, :].rearrange("p (a b) -> p a b", a=4), ALU.subtract).then_inc(vn, 1)
                else:
                    ve.wait_ge(ds_mm, k)
                    ve.wait_ge(ex_ready, i + 1)
                    if ph:
                        o = o_acc[:, heads, tile * P + 64 * cc:tile * P + 64 * cc + 64]
                        v.tensor_tensor(o, o, pS[0][:, 0:T].rearrange("p (h t) -> p h t", h=4), ALU.add)
                    for h in range(4 * q, 4 * q + 4):
                        last = v.scalar_tensor_tensor(state[d][:, h, :], state[d][:, h, :], ex[d][:, 3 + cc, h:h + 1],
                                                      pS[1][:, (h % 4) * P:(h % 4 + 1) * P], ALU.mult, ALU.add)
                    last.then_inc(s_upd, 1)

            def prepare(i, ph, tile, d):
                one_ = i + 1
                lb = glog[:, tile + 2 * ph, 16 * d + 8:16 * d + 16]
                pyf = pY[:, :, :].rearrange("p a (b c) -> p (a b) c", c=P)
                bank = lambda t_: t_[:, :].rearrange("p (a b) -> p a b", a=4)
                ve.wait_ge(small_mm, one_)
                c_ = pG[0][:, 0:8]
                v.tensor_scalar(neg_c, c_, -1.0, None, ALU.mult)
                link(v.tensor_copy(ex[d][:, 1], c_))
                v.tensor_tensor(ex[d][:, 0], c_, lb, ALU.add)
                v.tensor_copy(ex[d][:, 2], lb)
                v.tensor_copy(ex[d][:, 3:5], pG[0][:, 16:32].rearrange("p (a b) -> p a b", a=2))
                v.tensor_tensor(ex[d][:, 1], pG[0][:, 8:16], ex[d][:, 1], ALU.subtract).then_inc(expin, 1)
                ve.wait_ge(rb_mm, one_)
                v.tensor_tensor(BE, pyf[:, 0:HEADS, :], mask(M_STRICT + d), ALU.add).then_inc(be1, 1)
                if ph:
                    ve.wait_ge(r_mm, i - 3)
                    for q in range(2):
                        last = v.tensor_tensor(AE[d][q], pyf[:, 8 + 4 * q:12 + 4 * q, :], mask4(M_INCL + d), ALU.add)
                    last.then_inc(ae1, 1)
                ve.wait_ge(be2, one_)
                ve.wait_ge(kk_mm, one_)
                for q in range(2):
                    last = v.scalar_tensor_tensor(BE[:, 4 * q:4 * q + 4, :], bank(pS[q]), -1.0, BE[:, 4 * q:4 * q + 4, :], ALU.mult, ALU.mult)
                last.then_inc(b_ready, 1)
                ve.wait_ge(bt_mm, one_)
                link(v.tensor_tensor(ET, pyf[:, 0:HEADS, :], mask(M_LEV + d), ALU.mult))
                v.tensor_tensor(ET, ET, eye.to_broadcast([P, HEADS, P]), ALU.add).then_inc(e0, 1)
                if ph:
                    ve.wait_ge(ae2, i - 3)
                    ve.wait_ge(kq_mm, i - 3)
                    for q in range(2):
                        last = v.tensor_tensor(AE[d][q], AE[d][q], bank(pS[q]), ALU.mult)
                    last.then_inc(att, 1)
                for lv in range(5):
                    for q in range(2):
                        x = X[:, 4 * q:4 * q + 4, :]
                        ve.wait_ge(rp, 10 * i + 2 * lv + q + 1)
                        link(v.tensor_tensor(x, bank(pG[q]), mask4(M_LEV + 2 * (lv + 1) + d), ALU.mult))
                        v.tensor_tensor(x, x, eye.to_broadcast([P, 4, P]), ALU.add).then_inc(x_ready, 1)
                        if i and 2 * lv + q < 8:
                            scan_piece(i - 1, 2 * lv + q)
                ve.wait_ge(wu_mm, one_)
                v.tensor_copy(U_t[d], pyf[:, HEADS:, :]).then_inc(u_sb, 1)

            for i, body in enumerate(BODIES):
                if i == 4:
                    link(v.memset(o_acc, 0.0))
                prepare(i, *body)
            for stage in range(8):
                scan_piece(len(BODIES) - 1, stage)
            ve.wait_ge(o_std, 1)
            link(v.reciprocal(hn, hn))
            link(v.tensor_tensor(o_acc, o_acc, hn, ALU.mult))
            link(v.tensor_scalar(o_acc, o_acc, out_g[:, 0:1], None, ALU.mult))
            v.tensor_tensor(o_acc, o_acc, zs, ALU.mult).then_inc(o_norm, 1)
            h_low(4, o_acc)
            ve.wait_ge(lo_ready, KD + NKV + NIN + AHEAD + RING)
            with ve.Fori(0, NC // RING) as n:
                for j in range(RING):
                    split_lo(n, KD + NKV + NIN, j + AHEAD)
                    ve.wait_ge(block_done, RING * n + (KD + NKV + NIN + j + 1 + RING))
                    x = res[0][:, bass.ds(RING * n + j, 1), :].rearrange("p o t -> p (o t)")
                    v.scalar_tensor_tensor(x, pS[j % 2][:, 0:T], gate1[:, bass.ds(RING * n + j, 1)],
                                           x, ALU.mult, ALU.add).then_inc(evacuated, 1)
            ve.wait_ge(evacuated, E3 + 2)
            v.memset(mark[:, 6:7], 0.0).then_inc(y_res, NC)
            norm(6, res[0], 1, 1, 0)
            h_low(5, nrm)
            peer(2, K2, E3, True)
            ve.wait_ge(block_done, RING + K2 + L0)
            ve.wait_ge(res_in, 48)
            add_branch(4, res[0], y_chunk, 1, 5, 0, fin_ready)
            ve.wait_ge(std_ready, 8)
            link(v.reciprocal(inv_std, std))
            link(v.tensor_tensor(hn, res[0], inv_std.unsqueeze(1).to_broadcast([P, NC, T]), ALU.mult))
            v.tensor_tensor(nrm, hn, fin_g2[:, :].unsqueeze(2).to_broadcast([P, NC, T]), ALU.mult).then_inc(normed, 1)

        @block.gpsimd
        def _(pool):
            g_ = nc.gpsimd
            g_.iota(iota[:, :], pattern=[[1, P]], base=0, channel_multiplier=0,
                    allow_small_or_imprecise_dtypes=True).then_inc(ready, 1)
            pool.wait_ge(normed, 2)
            pool.dma_start(a["x_res"], res[0]).then_inc(spilled, 16)
            pool.dma_start(a["x_h"], nrm).then_inc(spilled, 16)
            pool.wait_ge(normed, 4)
            pool.dma_start(a["c_res"], res[1]).then_inc(spilled, 16)

            def peer(g):
                pool.wait_ge(h_split, (1, 2, 6)[g])
                pool.dma_start(keys, a["keysT"][g // 2]).then_inc(keys_in, 16)
                if g == 0:
                    pool.wait_ge(ready, 3)
                with pool.Fori(0, T // 8) as n:
                    for j in range(2):
                        pool.wait_ge(gates_sb, 2 * n + (64 * g + j + 3))
                        x = buf[:, :, bass.ds(8 * n + 4 * j, 4)]
                        g_.tensor_tensor(x, x, g4[j][:, :, :], ALU.mult).then_inc(gated, 1)
            g_.memset(pmark[:, :], 0.0).then_inc(gated, 2)
            pool.wait_ge(spilled, 48)
            peer(0)
            pool.wait_ge(block_done, RING + L0)
            pool.dma_start(hn, a["x_h"]).then_inc(h_in, 16)
            pool.dma_start(res[1], a["c_res"]).then_inc(res_in, 16)
            pool.wait_ge(fin_ready, 1)
            pool.dma_start(a["c_res"], res[1]).then_inc(spilled, 16)
            pool.wait_ge(spilled, 64)
            peer(1)
            pool.wait_ge(block_done, RING + KD)
            pool.dma_start(res[0], a["x_res"]).then_inc(res_in, 16)
            pool.dma_start(res[1], a["c_res"]).then_inc(c_in, 16)
            for dst, src in ((masks, a["masks"]), (cw, a["conv_wT"]), (w_ab, a["w_abT"]), (ab_c[:, 0:2], a["ab_rows"]),
                             (ab_c[:, 2], a["a_log"]), (out_g, a["out_gT"]), (fin_g2[:, :], a["final_gT"])):
                pool.dma_start(dst, src).then_inc(consts2_in, 16)

            pool.wait_ge(lo_ready, KD + AHEAD + RING)
            with pool.Fori(0, (NKV + NIN) // RING) as n:
                for j in range(RING):
                    slot = (j + AHEAD) % RING
                    pool.wait_ge(hi_ready, RING * n + (KD + j + AHEAD + 1))
                    g_.tensor_tensor(lo[slot][:, :, :], raw[slot][:, :, :], hi[slot][:, :, :].bitcast(F32), ALU.subtract).then_inc(lo_ready, 1)

            for i, (ph, tile, d) in enumerate(BODIES):
                pool.wait_ge(kv_sb, i + 1)
                pool.wait_ge(ex_ready, i + 1)
                bc = lambda j: ex[d][:, j].unsqueeze(2).to_broadcast([P, HEADS, P])
                g_.tensor_tensor(KG[d], K_t, bc(1), ALU.mult)
                pool.wait_ge(b_ready, i + 1)
                g_.tensor_tensor(E, BE, masks[:, M_LEV + 1 - d:M_LEV + 2 - d, :].to_broadcast([P, HEADS, P]), ALU.mult).then_inc(e_masked, 1)
                pool.wait_ge(e_masked, i + 1)
                g_.tensor_tensor(E, E, ident[:, :].unsqueeze(1).to_broadcast([P, HEADS, P]), ALU.add).then_inc(e_first, 1)
                if ph:
                    pool.wait_ge(er, i - 3)
                    g_.tensor_tensor(QG[d], QG[d], conv_x[:, 0:HEADS, tile * P:(tile + 1) * P], ALU.mult)
                g_.tensor_tensor(K_t, K_t, bc(0), ALU.mult)
                g_.tensor_tensor(V_t, V_t, bc(2), ALU.mult).then_inc(kvb, 1)
            pool.wait_ge(normed, 7)
            pool.dma_start(a["x_res"], res[0]).then_inc(spilled, 16)
            pool.wait_ge(spilled, 80)
            peer(2)
            pool.wait_ge(block_done, RING + K2 + L0)
            pool.dma_start(res[0], a["x_res"]).then_inc(res_in, 16)
            pool.wait_ge(normed, 8)
            pool.dma_start(out, nrm).then_inc(out_done, 16)
            pool.wait_ge(out_done, 16)

        @block.tensor
        def _(pe):
            t_ = nc.tensor
            pe.wait_ge(ready, 3)
            pe.wait_ge(silu_done, 1)
            cs = small[:, 160:160 + 2 * NC].rearrange("p (c b) -> p c b", b=2)
            t_.matmul(pS[0][:, 0:2], ones_mean, inv_d[:, :].to_broadcast([P, 2]), start=True, stop=True).then_inc(mod_done, MOD_RING)

            def adaln(L, g0, groups):
                def products(n, i):
                    for j in range(RING):
                        slot = RING * (i % 2) + j
                        pe.wait_ge(mod_in[slot], n * 16 + (L * N_GRP + g0 + i + 2) // 2 * 16)
                        for c in range(2):
                            mm = t_.matmul(pS[i % 2][0:2, :], cs[:, 2 * j + c, :], mod_slot(slot)[:, c, :],
                                           start=(j == 0 and c == 0), stop=(j == RING - 1 and c == 1))
                        mm.then_inc(mod_done, 1)

                def to_channels(n, i):
                    pe.wait_ge(row_ready, 2 * n + (L * N_GRP + g0 + i + 1))
                    for q in range(GRP // P):
                        col = 16 * n + (8 * (g0 + i) + 2 * q)
                        t_.matmul(pG[L][:, bass.ds(col, 2)], row[i][:, q * P:(q + 1) * P], ident[0:2, 0:2],
                                  start=True, stop=True, skip_group_check=True).then_inc(mods_T, 1)

                products(0, 0)
                with pe.Fori(0, groups // 2 - 1) as n:
                    products(n, 1)
                    to_channels(n, 0)
                    products(n, 2)
                    to_channels(n, 1)
                products(groups // 2 - 1, 1)
                to_channels(groups // 2 - 1, 0)
                to_channels(groups // 2 - 1, 1)

            adaln(0, 0, N_GRP)
            t_.matmul(pS[0][:, 0:2], ones_mean, inv_d[:, :].to_broadcast([P, 2]), start=True, stop=True).then_inc(block_done, RING)
            t_.matmul(pS[0][:, 0:2], ones_mean, inv_d[:, :].to_broadcast([P, 2]), start=True, stop=True).then_inc(evacuated, 2)
            t_.matmul(pS[0][:, 0:2], ones_mean, inv_d[:, :].to_broadcast([P, 2]), start=True, stop=True).then_inc(gates_mm, 4)

            def norm(k):
                pe.wait_ge(squares, k + 1)
                if k == 0:
                    pe.wait_ge(mod_ready, 1)
                for c in range(NC):
                    mm = t_.matmul(pG[0][:, 0:T], ones_mean, sq[:, c, :], start=(c == 0), stop=(c == NC - 1))
                mm.then_inc(mean_sq, 1)

            def pool_project(k):
                pe.wait_ge(pooled_ready, k + 1)
                for g in range(4):
                    for o in range(2):
                        for i in range(2):
                            mm = t_.matmul(pY[:, g, o * T:(o + 1) * T], pool_w[:, 4 * g + 2 * i + o, :], pooled[:, 2 * g + i, :],
                                           start=(i == 0), stop=(i == 1), skip_group_check=True)
                mm.then_inc(pool_mm, 1)

            def s_block(n, k0, e0, j, w=T):
                slot = (k0 + j) % RING
                out = pS[j % 2][:, 0:w]
                pe.wait_ge(lo_ready, RING * n + (k0 + j + 1 + RING))
                pe.wait_ge(evacuated, RING * n + (e0 + j + 1))
                for c in range(NC):
                    t_.matmul(out, hi[slot][:, c, :], h_hi[:, c, :], start=(c == 0), stop=False)
                    t_.matmul(out, hi[slot][:, c, :], h_lo[:, c, :], start=False, stop=False)
                    mm = t_.matmul(out, lo[slot][:, c, :], h_hi[:, c, :], start=False, stop=(c == NC - 1))
                mm.then_inc(block_done, 1)
                return mm

            def s_blocks(k, e, nb):
                with pe.Fori(0, nb // RING) as n:
                    for j in range(RING):
                        s_block(n, k, e, j)

            def peer(g, k0, e0, last):
                pe.wait_ge(h_split, (1, 2, 6)[g])
                s_blocks(k0, e0, NQ)
                pe.wait_ge(evacuated, 2 + e0 + NQ)
                pe.wait_ge(keys_in, 16 * (g + 1))
                if g == 1:
                    pe.wait_ge(fin_ready, 1)
                for r in range(NT):
                    if r:
                        pe.wait_ge(scores_read, NT * g + r)
                    for q in range(NQ):
                        mm = t_.matmul(pY[:, q // 4, (q % 4) * P:(q % 4 + 1) * P], qT[:, q, r * P:(r + 1) * P], keys[:, q, :],
                                       start=True, stop=True, skip_group_check=True)
                    mm.then_inc(scores_done, 1)
                s_blocks(k0 + NQ, e0 + NQ, NE)
                pe.wait_ge(picks_ready, g + 1)
                pe.wait_ge(gated, 2 + 64 * g)
                for q, (dst, off) in enumerate([(pG[0], 0), (pG[0], T), (pG[1], 0)]):
                    for r in range(NT):
                        mm = t_.transpose(dst[:, off + r * P:off + (r + 1) * P], picks[q][:, r * P:(r + 1) * P], ident[:, :])
                mm.then_inc(picksT, 1)
                with pe.Fori(0, N_OCT // 2) as n:
                    for k in range(4):
                        o, q = k // 2, k % 2
                        at_ = 4 * n + (2 * N_OCT * g + k + 1)
                        pe.wait_ge(onehot, at_)
                        pe.wait_ge(rows_gated, at_)
                        pe.wait_ge(gates_sb, at_)
                        for t in range(QUAD):
                            mm = t_.matmul(pG[q][:, t * P:(t + 1) * P], second_rows(o)[:, QUAD * q + t, :].bitcast(F32),
                                           gated1[:, 8 * o + QUAD * q + t, :], start=True, stop=True, skip_group_check=True)
                        mm.then_inc(gates_mm, 1)
                kv = k0 + NQ + NE
                def v_block(n, b0, j, first, lastb):
                    slot = (kv + j) % RING
                    pe.wait_ge(lo_ready, (RING * n + (kv + b0 + j + 1 + RING)) if n is not None else kv + b0 + j + 1 + RING)
                    pe.wait_ge(w_lo, (RING * n + (NE * g + b0 + j + 1)) if n is not None else NE * g + b0 + j + 1)
                    for c in range(NC):
                        o = pY[:, c // 2, (c % 2) * T:(c % 2) * T + T]
                        w1, w2 = h_hi[:, j, :], h_lo[:, j, :]
                        t_.matmul(o, hi[slot][:, c, :], w1, start=first and c % 2 == 0, stop=False, skip_group_check=True)
                        t_.matmul(o, hi[slot][:, c, :], w2, start=False, stop=False, skip_group_check=True)
                        mm = t_.matmul(o, lo[slot][:, c, :], w1, start=False, stop=lastb, skip_group_check=True)
                    mm.then_inc(block_done, 1)
                for j in range(RING):
                    v_block(None, 0, j, j == 0, False)
                with pe.Fori(0, NE // RING - 1) as n:
                    for j in range(RING):
                        v_block(n, RING, j, False, False)

            for k in range(2):
                norm(2 * k)
                adaln(1, k * N_GRP // 2, N_GRP // 2)
                pool_project(k)
                norm(2 * k + 1)
            peer(0, 0, 0, False)
            peer(1, L0, NQ + NE, False)

            def ab_project(k, first):
                pe.wait_ge(normed, 5 + k)
                for r in range(NT):
                    for c in range(NC):
                        mm = t_.matmul(pG[1][:, (2 * k + r) * 32:(2 * k + r + 1) * 32], nrm[:, c, r * P:(r + 1) * P], w_ab[:, c, :],
                                       start=(c == 0), stop=(c == NC - 1), skip_group_check=True)
                mm.then_inc(ab_mm, 1)

            pe.wait_ge(fin_ready, 2)
            pe.wait_ge(consts2_in, 16 * 7)
            norm(4)
            ab_project(0, True)
            pe.wait_ge(h_split, 3)
            s_blocks(KD, E2, NKV)
            norm(5)
            ab_project(1, False)
            pe.wait_ge(h_split, 4)
            s_blocks(KD + NKV, E2 + NKV, NIN)
            for r in range(3):
                pe.wait_ge(l2_sq, r + 1)
                if r:
                    pe.wait_ge(l2_std, r)
                for b in range(4):
                    mm = t_.matmul(pY[:, b, :], ones_mean, sq[:, 2 * b:2 * b + 2, :].rearrange("p a b -> p (a b)"), start=True, stop=True)
                mm.then_inc(l2_mm, 1)

            def scan_stage(i, stage):
                ph, tile, d = BODIES[i]
                st, q, second = stage // 4, (stage // 2) % 2, stage % 2
                k = 4 * i + stage // 2 + 1
                cc = st if d == 0 else 1 - st
                r = slice(64 * cc, 64 * cc + 64)
                if not second:
                    pe.wait_ge(s_upd, k)
                    for h in range(4 * q, 4 * q + 4):
                        mm = t_.matmul(pS[0][r, (h % 4) * P:(h % 4 + 1) * P], WT[d][:, h, r], state[d][:, h, :], start=True, stop=True, skip_group_check=True)
                    mm.then_inc(ws_mm, 1)
                else:
                    pe.wait_ge(vn, k)
                    for h in range(4 * q, 4 * q + 4):
                        if ph:
                            o = pS[0][:, 64 * (h % 4):64 * (h % 4) + 64]
                            t_.matmul(o, state[d][:, h, :], QG[d][:, h, r], start=True, stop=False, skip_group_check=True)
                            t_.matmul(o, U_t[d][r, h, :], AE[d][q][r, h % 4, r], start=False, stop=True, skip_group_check=True)
                        mm = t_.matmul(pS[1][:, (h % 4) * P:(h % 4 + 1) * P], KG[d][r, h, :], U_t[d][r, h, :], start=True, stop=True, skip_group_check=True)
                    mm.then_inc(ds_mm, 1)

            def prepare(i, ph, tile, d):
                one_ = i + 1
                kx, vx = (conv_c[:, 0:HEADS], conv_c[:, HEADS:]) if ph == 0 else (conv_x[:, HEADS:2 * HEADS], conv_x[:, 2 * HEADS:])
                cols = slice(tile * P, (tile + 1) * P)
                g_ = glog[:, tile + 2 * ph, 16 * d:16 * d + 8]
                lb = glog[:, tile + 2 * ph, 16 * d + 8:16 * d + 16]
                pyf = pY[:, :, :].rearrange("p a (b c) -> p (a b) c", c=P)
                psf = [pS[h // 4][:, (h % 4) * P:(h % 4 + 1) * P] for h in range(HEADS)]
                for j, m in enumerate((M_CUM + d, M_CHUNK, M_SEG, M_SEG + 1)):
                    mm = t_.matmul(pG[0][:, 8 * j:8 * j + 8], masks[:, m, :], g_, start=True, stop=True, skip_group_check=True)
                mm.then_inc(small_mm, 1)
                for h in range(HEADS):
                    mm = t_.matmul(psf[h], kx[:, h, cols], kx[:, h, cols], start=True, stop=True, skip_group_check=True)
                mm.then_inc(kk_mm, 1)
                if i:
                    pe.wait_ge(wt_sb, i)
                    pe.wait_ge(u_sb, i)
                for h in range(HEADS):
                    t_.transpose(pyf[:, h, :], kx[:, h, cols], ident[:, :])
                    mm = t_.transpose(pyf[:, HEADS + h, :], vx[:, h, cols], ident[:, :])
                mm.then_inc(trans_mm, 1)
                pe.wait_ge(kv_sb, one_)
                for h in range(HEADS):
                    t_.matmul(pyf[:, h, :], g_[:, h:h + 1].to_broadcast([P, P]), masks[:, M_CUM + d, :], start=True, stop=False, skip_group_check=True)
                    mm = t_.matmul(pyf[:, h, :], lb[:, h:h + 1].to_broadcast([P, P]), ident[:, :], start=False, stop=True, skip_group_check=True)
                mm.then_inc(rb_mm, 1)
                if ph:
                    for h in range(HEADS):
                        mm = t_.matmul(pyf[:, HEADS + h, :], g_[:, h:h + 1].to_broadcast([P, P]), masks[:, M_CUM + d, :], start=True, stop=True, skip_group_check=True)
                    mm.then_inc(r_mm, 1)
                pe.wait_ge(b_ready, one_)
                for h in range(HEADS):
                    mm = t_.transpose(pyf[:, h, :], BE[:, h, :], ident[:, :])
                mm.then_inc(bt_mm, 1)
                if ph:
                    for h in range(HEADS):
                        mm = t_.matmul(psf[h], kx[:, h, cols], conv_x[:, h, cols], start=True, stop=True, skip_group_check=True)
                    mm.then_inc(kq_mm, 1)
                pe.wait_ge(e0, one_)
                for lv in range(5):
                    for q in range(2):
                        if lv:
                            pe.wait_ge(e_sb, 10 * i + 2 * (lv - 1) + q + 1)
                        for h in range(4 * q, 4 * q + 4):
                            mm = t_.matmul(pG[q][:, (h % 4) * P:(h % 4 + 1) * P], BE[:, h, :], ET[:, h, :], start=True, stop=True, skip_group_check=True)
                        mm.then_inc(rp, 1)
                        if i and 2 * lv + q < 8:
                            if ph and 2 * lv + q == 0:
                                pe.wait_ge(att, i - 3)
                            scan_stage(i - 1, 2 * lv + q)
                    if lv == 0:
                        pe.wait_ge(e_first, one_)
                        if ph:
                            pe.wait_ge(er, i - 3)
                    for q in range(2):
                        pe.wait_ge(x_ready, 10 * i + 2 * lv + q + 1)
                        for h in range(4 * q, 4 * q + 4):
                            mm = t_.matmul(pyf[:, h, :], X[:, h, :], E[:, h, :], start=True, stop=True, skip_group_check=True)
                            if lv < 4:
                                mm = t_.matmul(pyf[:, HEADS + h, :], E[:, h, :], X[:, h, :], start=True, stop=True, skip_group_check=True)
                        mm.then_inc(e_mm, 1)
                pe.wait_ge(e_sb, 10 * i + 10)
                pe.wait_ge(kvb, one_)
                for h in range(HEADS):
                    t_.matmul(pyf[:, h, :], K_t[:, h, :], E[:, h, :], start=True, stop=True, skip_group_check=True)
                    mm = t_.matmul(pyf[:, HEADS + h, :], E[:, h, :], V_t[:, h, :], start=True, stop=True, skip_group_check=True)
                mm.then_inc(wu_mm, 1)
                if i:
                    pe.wait_ge(s_upd, 4 * i + 1)

            pe.wait_ge(gl_done, 1)
            for i, body in enumerate(BODIES):
                prepare(i, *body)
            pe.wait_ge(wt_sb, len(BODIES))
            pe.wait_ge(u_sb, len(BODIES))
            for stage in range(8):
                scan_stage(len(BODIES) - 1, stage)
            pe.wait_ge(o_sq, 1)
            for b in range(4):
                mm = t_.matmul(pY[:, b, :], ones_mean, sq[:, 2 * b:2 * b + 2, :].rearrange("p a b -> p (a b)"), start=True, stop=True)
            mm.then_inc(o_mm, 1)
            pe.wait_ge(h_split, 5)
            s_blocks(KD + NKV + NIN, E3 - NC, NC)
            norm(6)
            peer(2, K2, E3, True)
            norm(7)


def blocks_of(m):
    return m.reshape(NC, P, -1, P).transpose(2, 1, 0, 3)


def chan(v):
    return np.moveaxis(v.reshape(v.shape[:-1] + (NC, P)), -1, 0)


def chunk_masks():
    r, c = np.arange(P)[:, None], np.arange(P)[None, :]
    same = r // 64 == c // 64
    z = np.zeros((P, P))
    m = [same & (r <= c), same & (r >= c), same, (r < 64) | (z > 0), (r >= 64) | (z > 0)]
    m += [np.where(x, 0.0, -1e30) for x in (same & (r < c), same & (r > c), same & (r <= c), same & (r >= c))]
    for lv in range(6):
        s = 2 ** lv
        x = (r // (2 * s) == c // (2 * s)) & (r % (2 * s) >= s) & (c % (2 * s) < s)
        m += [x, x.T]
    return np.ascontiguousarray(np.stack([np.asarray(x, np.float32) for x in m], 1))


def inverse_counts():
    out = np.zeros((2 * NC, T), np.float32)

    def line(n, w):
        t = np.arange(n)
        return np.clip(t - w // 2 + w, 0, n) - np.clip(t - w // 2, 0, n)
    for g, w in enumerate(WINDOWS):
        out[2 * g:2 * g + 2] = (1.0 / (line(ROWS, w)[:, None] * line(GRID_W, w)[None, :])).reshape(-1)
        out[NC + 2 * g:NC + 2 * g + 2] = 1.0 / line(T, w)
    return np.ascontiguousarray(np.broadcast_to(out, (P, 2 * NC, T)))


def kernel(**x):
    import concourse.bacc as bacc
    from concourse.bass_utils import run_bass_kernel_spmd
    x = {k: np.asarray(v) for k, v in x.items()}
    f = np.ascontiguousarray
    peer = [np.concatenate([blocks_of(x["peer_wq"][L]), blocks_of(x["peer_u"][L].T),
                            x["peer_v"][L].reshape(NE, P, NC, P)]) for L in range(DEPTH)]
    sign = np.broadcast_to(np.array([1, -1], np.float32)[None, :, None], (2, 2, HEADS)).reshape(-1)
    bias = np.stack([x["dn_dt_bias"][0], np.zeros((2, HEADS), np.float32)], 1).reshape(-1)
    alog = np.stack([x["dn_a_log"][0], np.zeros((2, HEADS), np.float32)], 1).reshape(-1)
    arrays = {
        "ident": np.eye(P, dtype=np.float32),
        "cT": f(chan(np.stack([x["c"][0], x["c_ctx"]])).transpose(0, 2, 1).reshape(P, 2 * NC)),
        "mod_bT": f(np.moveaxis(x["mod_b"].reshape(DEPTH * NMOD, P), 1, 0)),
        "gainT": f(chan(np.stack([x["norm1_g"], x["norm2_g"]], 1)).reshape(P, -1)),
        "pool_scaleT": f(chan(x["pool_scale"][0])),
        "xT": f(chan(x["x"][0]).transpose(0, 2, 1)),
        "ctxT": f(chan(x["ctx"][0]).transpose(0, 2, 1)),
        "counts": inverse_counts(),
        "pool_wT": f(x["pool_w"][0].reshape(4, 2, P, 2, P).transpose(2, 0, 1, 3, 4).reshape(P, 16, P)),
        "mod_wT": f(x["mod_w"].reshape(DEPTH, RING, 2, P, N_GRP, GRP).transpose(0, 4, 1, 3, 2, 5).reshape(-1, P, 2, GRP)),
        "keysT": f(x["peer_keys"].reshape(DEPTH, NQ, NKEYS, P).transpose(0, 3, 1, 2)),
        "masks": chunk_masks(),
        "conv_wT": f(x["dn_conv_w"][0].reshape(5, 3 * HEADS, P).transpose(2, 0, 1)),
        "w_abT": f(x["dn_w_in"][0][:, 4 * D:].reshape(NC, P, 4 * HEADS).transpose(1, 0, 2)),
        "ab_rows": f(np.broadcast_to(np.stack([sign, bias]), (P, 2, 4 * HEADS))),
        "a_log": f(np.broadcast_to(alog, (P, 4 * HEADS))),
        "out_gT": f(x["dn_norm_g"][0].reshape(P, 1)),
        "final_gT": f(chan(x["final_g"])),
        "blocks": f(np.concatenate([peer[0], blocks_of(x["dn_w_in"][0][:, :4 * D]), blocks_of(x["dn_w_out"][0]), peer[1]])),
    }
    nc = bacc.Bacc("TRN2", target_bir_lowering=False, num_devices=1)
    aps = {k: nc.dram_tensor("in_" + k, v.shape, mybir.dt.from_np(v.dtype), kind="ExternalInput").ap() for k, v in arrays.items()}
    for k in ("x_res", "x_h", "c_res"):
        aps[k] = nc.dram_tensor("spill_" + k, (P, NC, T), F32, kind="Internal").ap()
    out = nc.dram_tensor("out", (P, NC, T), F32, kind="ExternalOutput").ap()
    build(nc, aps, out)
    r = run_bass_kernel_spmd(nc, [{"in_" + k: v for k, v in arrays.items()}], core_ids=[0]).results[0]
    return np.ascontiguousarray(np.asarray(r["out"]).transpose(2, 1, 0).reshape(1, T, D))
```
